# Optimizing a Trainium2 kernel written in Bass

```python
import jax, jax.numpy as jnp
from jax import lax
import numpy as np

D_MODEL = 1024
BATCH = 1
SEQ = 512
DEPTH = 2

D_MIX = D_MODEL
N_MIXERS = 4
GROUP_WIDTH = D_MIX // N_MIXERS
N_GROUP_HEADS = 4
HEAD_DIM = GROUP_WIDTH // N_GROUP_HEADS
N_IN_SLICES = 10
D_IN = N_IN_SLICES * GROUP_WIDTH
LRU_CONV = 4
LRU_C = 8.0
HGRN_CHUNK = 64
POOL_WINDOWS = (2, 4, 8, 16)
SCONV_WIDTH = 3
D_FF = 2816
N_EXPERTS = 8
TOP_K = 2
D_FF_EXPERT = 3584
ROW_BLOCK = 128
NORM_EPS = 1e-6
HEAD_NORM_EPS = 1e-5
N_DENSE = (DEPTH + 1) // 2
N_MOE = DEPTH // 2

kernel_name = 'hybrid_lru_hgrn2_pool_sconv_moe'

F32 = jnp.float32

def rms_norm(x, g):
    xf = x.astype(F32)
    y = xf * lax.rsqrt(jnp.mean(xf * xf, axis=-1, keepdims=True) + NORM_EPS)
    return (y * g.astype(F32)).astype(x.dtype)

def causal_depthwise_conv(x, w):
    k = w.shape[0]
    return lax.conv_general_dilated(
        x, w[:, None, :].astype(x.dtype), window_strides=(1,), padding=[(k - 1, 0)],
        dimension_numbers=('NWC', 'WIO', 'NWC'), feature_group_count=x.shape[-1])

def block_diag_linear(x, w, b):
    bsz, s, c = x.shape
    xh = x.reshape(bsz, s, N_GROUP_HEADS, HEAD_DIM)
    return jnp.einsum('bshi,hij->bshj', xh, w).reshape(bsz, s, c) + b

def rg_lru(x, w_a, b_a, w_x, b_x, lam):
    r = jax.nn.sigmoid(block_diag_linear(x, w_a, b_a).astype(F32))
    i = jax.nn.sigmoid(block_diag_linear(x, w_x, b_x).astype(F32))
    log_a = -LRU_C * r * jax.nn.softplus(-lam.astype(F32))
    a = jnp.exp(log_a)
    mult = jnp.sqrt(-jnp.expm1(2.0 * log_a))
    u = mult * i * x.astype(F32)

    def combine(c1, c2):
        a1, b1 = c1
        a2, b2 = c2
        return a1 * a2, a2 * b1 + b2

    _, h = lax.associative_scan(combine, (a, u), axis=1)
    return h.astype(x.dtype)

def hgrn2(q, f_pre, v, g, lb, norm_g):
    bsz, s, c = q.shape
    n_chunks = s // HGRN_CHUNK
    z = f_pre.astype(F32)
    log_f = jnp.log(lb + (1.0 - lb) * jax.nn.sigmoid(z))
    k = (1.0 - lb) * jax.nn.sigmoid(-z)
    qf = jax.nn.silu(q.astype(F32))

    def to_chunks(t):
        return t.reshape(bsz, n_chunks, HGRN_CHUNK, N_GROUP_HEADS, HEAD_DIM).transpose(1, 0, 3, 2, 4)

    qc, kc, vc, gc = (to_chunks(t) for t in (qf, k, v.astype(F32), log_f))
    causal = jnp.tril(jnp.ones((HGRN_CHUNK, HGRN_CHUNK), dtype=bool))

    def step(state, inp):
        q_, k_, v_, g_ = inp
        G = jnp.cumsum(g_, axis=2)
        diff = G[:, :, :, None, :] - G[:, :, None, :, :]
        decay = jnp.exp(jnp.where(causal[:, :, None], diff, -jnp.inf))
        scores = jnp.einsum('bhtk,bhtsk,bhsk->bhts', q_, decay, k_)
        o = (jnp.einsum('bhts,bhsv->bhtv', scores, v_)
             + jnp.einsum('bhtk,bhkv->bhtv', q_ * jnp.exp(G), state))
        G_last = G[:, :, -1:, :]
        state = (jnp.exp(G_last[:, :, 0, :])[..., None] * state
                 + jnp.einsum('bhsk,bhsv->bhkv', k_ * jnp.exp(G_last - G), v_))
        return state, o

    s0 = jnp.zeros((bsz, N_GROUP_HEADS, HEAD_DIM, HEAD_DIM), F32)
    _, o = lax.scan(step, s0, (qc, kc, vc, gc))
    o = o.transpose(1, 0, 3, 2, 4).reshape(bsz, s, N_GROUP_HEADS, HEAD_DIM)
    o = o * lax.rsqrt(jnp.mean(o * o, axis=-1, keepdims=True) + HEAD_NORM_EPS) * norm_g.astype(F32)
    o = o * jax.nn.silu(g.astype(F32).reshape(bsz, s, N_GROUP_HEADS, HEAD_DIM))
    return o.reshape(bsz, s, c).astype(q.dtype)

def multiscale_pool(x, w_pool, scale):
    bsz, s, c = x.shape
    xf = x.astype(F32).reshape(bsz, s, len(POOL_WINDOWS), HEAD_DIM)
    cs = jnp.cumsum(xf, axis=1)
    pos = jnp.arange(1, s + 1, dtype=F32)
    outs = []
    for gi, w in enumerate(POOL_WINDOWS):
        cg = cs[:, :, gi]
        lag = jnp.pad(cg[:, :-w], ((0, 0), (w, 0), (0, 0)))
        mean = (cg - lag) / jnp.minimum(pos, float(w))[None, :, None]
        outs.append(mean - xf[:, :, gi])
    d = jnp.stack(outs, axis=2).astype(x.dtype)
    y = jnp.einsum('bsgi,gij->bsgj', d, w_pool).reshape(bsz, s, c)
    return y * scale

def hybrid_mixer(h, w_in, w_out, lru_conv_w, lru_conv_b, lru_w_a, lru_b_a, lru_w_x, lru_b_x,
                 lru_lambda, lb, hgrn_norm_g, pool_w, pool_scale, sconv_w):
    proj = h @ w_in
    a_x, a_g, q, f, v, o_g, p, sb, sc, sx = jnp.split(proj, N_IN_SLICES, axis=-1)
    a_in = causal_depthwise_conv(a_x, lru_conv_w) + lru_conv_b
    y_a = rg_lru(a_in, lru_w_a, lru_b_a, lru_w_x, lru_b_x, lru_lambda) * jax.nn.gelu(a_g)
    y_b = hgrn2(q, f, v, o_g, lb, hgrn_norm_g)
    y_c = multiscale_pool(p, pool_w, pool_scale)
    y_d = sb * causal_depthwise_conv(sc * sx, sconv_w)
    y = jnp.concatenate([y_a, y_b, y_c, y_d], axis=-1)
    return y @ w_out

def swiglu(h, w_gate, w_up, w_down):
    return (jax.nn.silu(h @ w_gate) * (h @ w_up)) @ w_down

def moe_swiglu(h, w_router, w1, w3, w2):
    bsz, s, d = h.shape
    n = bsz * s
    xf = h.reshape(n, d)
    logits = jnp.dot(xf.astype(F32), w_router.astype(F32))
    top_logit, top_e = lax.top_k(logits, TOP_K)
    gates = jax.nn.softmax(top_logit, axis=-1)
    e_flat = top_e.reshape(-1).astype(jnp.int32)
    tok_flat = jnp.arange(n * TOP_K, dtype=jnp.int32) // TOP_K
    g_flat = gates.reshape(-1)
    order = jnp.argsort(e_flat)
    e_sorted, tok_sorted, g_sorted = e_flat[order], tok_flat[order], g_flat[order]
    counts = jnp.bincount(e_flat, length=N_EXPERTS)
    start = jnp.cumsum(counts) - counts
    padded = (counts + ROW_BLOCK - 1) // ROW_BLOCK * ROW_BLOCK
    pend = jnp.cumsum(padded)
    pstart = pend - padded
    dest = pstart[e_sorted] + (jnp.arange(n * TOP_K, dtype=jnp.int32) - start[e_sorted])
    n_blocks = (n * TOP_K + ROW_BLOCK - 1) // ROW_BLOCK + N_EXPERTS
    n_rows = n_blocks * ROW_BLOCK
    row_tok = jnp.full((n_rows,), n, jnp.int32).at[dest].set(tok_sorted)
    row_gate = jnp.zeros((n_rows,), F32).at[dest].set(g_sorted)
    block_e = jnp.minimum(
        jnp.searchsorted(pend, jnp.arange(n_blocks, dtype=pend.dtype) * ROW_BLOCK, side='right'),
        N_EXPERTS - 1)
    x_rows = jnp.concatenate([xf, jnp.zeros((1, d), xf.dtype)], axis=0)[row_tok]
    x_rows = x_rows.reshape(n_blocks, ROW_BLOCK, d)

    def expert_block(args):
        xb, e = args
        return (jax.nn.silu(xb @ w1[e]) * (xb @ w3[e])) @ w2[e]

    y_rows = lax.map(expert_block, (x_rows, block_e)).reshape(n_rows, d)
    y = jax.ops.segment_sum(y_rows.astype(F32) * row_gate[:, None], row_tok, num_segments=n + 1)[:n]
    return y.reshape(bsz, s, d).astype(h.dtype)

def setup_inputs(seed: int = 0) -> dict:
    key = jax.random.key(seed)
    ks = jax.random.split(key, 32)

    def nrm(k, shape, fan_in):
        return jax.random.normal(k, shape, F32) * (fan_in ** -0.5)

    u = jax.random.uniform(ks[9], (DEPTH, GROUP_WIDTH), F32, minval=0.9, maxval=0.999)
    a0 = u ** (1.0 / LRU_C)
    lru_lambda = jnp.log(a0) - jnp.log1p(-a0)
    return {
        'x': jax.random.normal(ks[0], (BATCH, SEQ, D_MODEL), F32),
        'w_in': nrm(ks[1], (DEPTH, D_MODEL, D_IN), D_MODEL),
        'w_out': nrm(ks[2], (DEPTH, D_MIX, D_MODEL), D_MIX),
        'lru_conv_w': nrm(ks[3], (DEPTH, LRU_CONV, GROUP_WIDTH), LRU_CONV),
        'lru_conv_b': 0.01 * jax.random.normal(ks[4], (DEPTH, GROUP_WIDTH), F32),
        'lru_w_a': nrm(ks[5], (DEPTH, N_GROUP_HEADS, HEAD_DIM, HEAD_DIM), HEAD_DIM),
        'lru_b_a': 0.01 * jax.random.normal(ks[6], (DEPTH, GROUP_WIDTH), F32),
        'lru_w_x': nrm(ks[7], (DEPTH, N_GROUP_HEADS, HEAD_DIM, HEAD_DIM), HEAD_DIM),
        'lru_b_x': 0.01 * jax.random.normal(ks[8], (DEPTH, GROUP_WIDTH), F32),
        'lru_lambda': lru_lambda,
        'hgrn_lower_bounds': 0.1 * jax.random.normal(ks[10], (DEPTH, GROUP_WIDTH), F32),
        'hgrn_norm_g': 1.0 + 0.02 * jax.random.normal(ks[11], (DEPTH, HEAD_DIM), F32),
        'pool_w': nrm(ks[12], (DEPTH, len(POOL_WINDOWS), HEAD_DIM, HEAD_DIM), HEAD_DIM),
        'pool_scale': 1.0 + 0.1 * jax.random.normal(ks[13], (DEPTH, GROUP_WIDTH), F32),
        'sconv_w': nrm(ks[14], (DEPTH, SCONV_WIDTH, GROUP_WIDTH), SCONV_WIDTH),
        'norm_mix_g': 1.0 + 0.02 * jax.random.normal(ks[15], (DEPTH, D_MODEL), F32),
        'norm_ffn_g': 1.0 + 0.02 * jax.random.normal(ks[16], (DEPTH, D_MODEL), F32),
        'ffn_w_gate': nrm(ks[17], (N_DENSE, D_MODEL, D_FF), D_MODEL),
        'ffn_w_up': nrm(ks[18], (N_DENSE, D_MODEL, D_FF), D_MODEL),
        'ffn_w_down': nrm(ks[19], (N_DENSE, D_FF, D_MODEL), D_FF),
        'moe_w_router': nrm(ks[20], (N_MOE, D_MODEL, N_EXPERTS), D_MODEL),
        'moe_w1': nrm(ks[21], (N_MOE, N_EXPERTS, D_MODEL, D_FF_EXPERT), D_MODEL),
        'moe_w3': nrm(ks[22], (N_MOE, N_EXPERTS, D_MODEL, D_FF_EXPERT), D_MODEL),
        'moe_w2': nrm(ks[23], (N_MOE, N_EXPERTS, D_FF_EXPERT, D_MODEL), D_FF_EXPERT),
        'final_norm_g': 1.0 + 0.02 * jax.random.normal(ks[24], (D_MODEL,), F32),
    }

def reference(x, w_in, w_out, lru_conv_w, lru_conv_b, lru_w_a, lru_b_a, lru_w_x, lru_b_x,
              lru_lambda, hgrn_lower_bounds, hgrn_norm_g, pool_w, pool_scale, sconv_w,
              norm_mix_g, norm_ffn_g, ffn_w_gate, ffn_w_up, ffn_w_down,
              moe_w_router, moe_w1, moe_w3, moe_w2, final_norm_g):
    lb_all = jnp.cumsum(jax.nn.softmax(hgrn_lower_bounds.astype(F32), axis=0), axis=0)
    lb_all = lb_all - lb_all[0]
    h = x
    for layer in range(DEPTH):
        hn = rms_norm(h, norm_mix_g[layer])
        h = h + hybrid_mixer(hn, w_in[layer], w_out[layer], lru_conv_w[layer], lru_conv_b[layer],
                             lru_w_a[layer], lru_b_a[layer], lru_w_x[layer], lru_b_x[layer],
                             lru_lambda[layer], lb_all[layer], hgrn_norm_g[layer],
                             pool_w[layer], pool_scale[layer], sconv_w[layer])
        hn = rms_norm(h, norm_ffn_g[layer])
        if layer % 2 == 0:
            j = layer // 2
            h = h + swiglu(hn, ffn_w_gate[j], ffn_w_up[j], ffn_w_down[j])
        else:
            j = layer // 2
            h = h + moe_swiglu(hn, moe_w_router[j], moe_w1[j], moe_w3[j], moe_w2[j])
    return rms_norm(h, final_norm_g)


_drawn_inputs = setup_inputs


def setup_inputs(seed=0):
    import zlib

    import numpy as np

    out = dict(_drawn_inputs(seed))
    spreads = {}
    factors = {'lru_b_a': 46.381,
     'lru_b_x': 50.467,
     'hgrn_lower_bounds': 4.547,
     'hgrn_norm_g': 3.12,
     'final_norm_g': 8.139}
    for name, (base, spread) in spreads.items():
        noise = np.random.default_rng([zlib.crc32(name.encode()), seed]).standard_normal(out[name].shape)
        drawn = base * np.exp(spread * noise) if base else spread * noise
        out[name] = __import__('jax').numpy.asarray(drawn.astype(out[name].dtype))
    for name, factor in factors.items():
        out[name] = (out[name] * factor).astype(out[name].dtype)
    return out
```

```python
from contextlib import ExitStack

import numpy as np

import concourse.bass as bass
from concourse import mybir

F32 = mybir.dt.float32
F32R = mybir.dt.float32r
I32 = mybir.dt.int32
U32 = mybir.dt.uint32
U8 = mybir.dt.uint8
ALU = mybir.AluOpType
ACT = mybir.ActivationFunctionType
AX = mybir.AxisListType

P = 128
D = 1024
KT = D // P
T = 512
NT = T // P
DEPTH = 2
GW = 256
CT = GW // P
NH = 4
HD = 64
FF = 2816
NE = 8
FE = 3584
EPS = 1e-6
HEAD_EPS = 1e-5
PIECE = 2048

A_X, A_G, Q, FG, V, O_G, PL, SB, SC, SX = range(10)
ORDER = [FG, Q, V, A_X, O_G, A_G, SC, SX, SB, PL]
N_IN = len(ORDER)
N_OUT = D // GW
DC = FF // GW
DENSE0 = N_IN + N_OUT
LAYER1 = DENSE0 + 3 * DC
MOE0 = LAYER1 + N_IN + N_OUT
CW = 512
EC = FE // CW
ROWS = 2 * P
MAX_ITEMS = (2 * T + NE * (ROWS - 1)) // ROWS
MIN_ITEMS = 2 * T // T * 2
LEVELS = 8

RING = [(s, u) for s in ORDER[:6] for u in range(2)] + [("gate", u) for u in range(4)] \
    + [(s, u) for s in ORDER[6:] for u in range(2)] + [("pool", u) for u in range(2)]

COLS = {}
_at = 0
for _name, _n in (("conv_w", 8), ("conv_b", 2), ("b_a", 2), ("b_x", 2), ("lam", 2), ("hlb", 4),
                  ("pool_scale", 2), ("sconv_w", 6), ("ramp", 32), ("norm_g", 256),
                  ("bd_a", 256), ("bd_x", 256), ("bd_p", 256)):
    COLS[_name] = _at
    _at += _n
NPAR = _at
MC_ONES, MC_LOWER, MC_IOTA, MC_ZERO, MC_TOK, MC_N, MC_E = 0, 128, 256, 264, 272, 276, 404
NMC = 404 + 8


def build(nc, x, w_in, w_out, w_gate, w_up, w_down, w_router, w1, w3, w2, norm_rows, params, ident,
          masks, moe_const, zeros, out):
    ctx = ExitStack()
    with ctx:
        base = [(nc.sbuf_base + 63) // 64 * 64]

        def at(name, shape, dt, offset):
            return nc.alloc_sbuf_tensor_at(name, shape, dt, offset=offset)

        def size(shape, dt):
            n = 1
            for s in shape[1:]:
                n *= s
            return (n * (1 if dt == U8 else 4) + 31) // 32 * 32

        def sb(name, shape, dt=F32):
            t = at(name, shape, dt, base[0])
            base[0] += size(shape, dt)
            return t

        def sem(name):
            return ctx.enter_context(nc.semaphore(name))

        raw = sb("raw", [P, 3, PIECE])
        w_his = sb("w_hi", [P, 3, PIECE], F32R)
        w_los = sb("w_lo", [P, 3, PIECE], F32R)
        h = sb("h", [P, NT, D])
        acts0 = base[0]
        act_hi = sb("act_hi", [P, KT, T], F32R)
        act_lo = sb("act_lo", [P, KT, T], F32R)
        idt = sb("idt", [P, P])
        mask = sb("mask", [P, LEVELS, P], U8)
        par = sb("par", [P, NPAR])
        state = sb("state", [P, NT, CT, HD])
        small = sb("small", [P, 96])
        ssq, var, rstd = small[:, 0:4], small[:, 4:8], small[:, 8:12]
        coef = small[:, 12:14]
        lbs = small[:, 14:16]
        omlb = small[:, 16:18]
        eg_last = small[:, 18:26].rearrange("p (c n) -> p c n", c=CT)
        o_ssq, o_var, o_rstd = small[:, 26:42], small[:, 42:58], small[:, 58:74]
        tmp = small[:, 74:96]

        mix0 = base[0]
        full = [P, CT, T]
        keys = sb("keys", full)
        decay = sb("decay", full)
        qf = sb("qf", full)
        ex = [sb(f"ex{i}", full) for i in range(2)]
        xs = [sb(f"xs{i}", full) for i in range(2)]
        scores = sb("scores", [P, NH, NT, P])
        vals = sb("vals", [P, NT, GW])
        ogate = sb("ogate", [P, NT, GW])
        lru_in = sb("lru_in", [P, CT, T + 16])
        w1b = sb("win1", [P, CT, T + 16])
        w2b = sb("win2", [P, CT, T + 16])
        agate = sb("agate", full)
        igate = sb("igate", full)
        mult = sb("mult", full)
        scv = sb("scv", full)
        sxv = sb("sxv", [P, CT, T + 2])
        assert base[0] <= nc.sbuf_usable_end, (base[0], nc.sbuf_usable_end)
        grow = xs[0].rearrange("p c t -> p (c t)")
        rows = [e.rearrange("p c t -> p (c t)") for e in ex]
        x_in = w1b[:, :, 0:T]
        r_gate = w2b[:, :, 0:T]
        tanh_l = lru_in[:, :, 0:T]

        d0 = mix0
        silu_d = at("silu_d", [P, 2, T], F32, d0)
        hid_d = at("hid_d", [P, 2, T], F32, d0 + 4096)
        hid_hi = at("hid_hi", [P, 2, T], F32R, d0 + 8192)
        o = (mix0 + 7 * 4096)
        hid_lo = at("hid_lo", [P, 2, T], F32R, o)

        base[0] = acts0
        xt_hi = sb("xt_hi", [P, 2, KT, P], F32R)
        xt_lo = sb("xt_lo", [P, 2, KT, P], F32R)
        silu_e = sb("silu_e", [P, 2, CW])
        hid_e = sb("hid_e", [P, 2, CW])
        ht_hi = sb("ht_hi", [P, 2, 4, P], F32R)
        ht_lo = sb("ht_lo", [P, 2, 4, P], F32R)
        assert base[0] <= acts0 + 32768
        base[0] = mix0
        w_hi2 = sb("w_hi2", [P, 3, PIECE], F32R)
        w_lo2 = sb("w_lo2", [P, 3, PIECE], F32R)
        comb = [at(f"comb{i}", [P, D], F32, mix0 + i * 4096) for i in range(8)]
        yacc = sb("yacc", [P, 2, D])
        xg = [sb(f"xg{i}", [P, D]) for i in range(2)]
        growf = sb("growf", [P, D])
        mcon = sb("mcon", [P, NMC])
        wr = sb("wr", [P, KT, NE])
        idx = sb("idx", [P, 2 * MAX_ITEMS + 2], U32)
        col = sb("col", [P, 2], U32)
        slots = sb("slots", [P, NT, 2], U32)
        tokens = sb("tokens", [P, NT], U32)
        items = sb("items", [1, 48], I32)
        rt = sb("rt", [P, 20, NT * NE])
        rtw = sb("rtw", [1, 5, 128])
        assert base[0] <= nc.sbuf_usable_end

        ps = ctx.enter_context(nc.psum_tensor("ps", [P, 8, 512], F32))

        hn_dram = nc.dram_tensor("hn_rows", (T, D), F32, kind="Internal").ap()
        y_dram = nc.dram_tensor("y_rows", (MAX_ITEMS * ROWS, D), F32, kind="Internal").ap()
        idx_dram = nc.dram_tensor("row_tokens", ((2 * MAX_ITEMS + 2) * P, 1), U32, kind="Internal").ap()

        raw_loaded = [sem(f"raw_loaded{i}") for i in range(3)]
        w_hi_done = sem("w_hi_done")
        w_lo_done = sem("w_lo_done")
        w_used = sem("w_used")
        const_loaded = sem("const_loaded")
        masks_loaded = sem("masks_loaded")
        mask_ready = sem("mask_ready")
        par_loaded = sem("par_loaded")
        grow_loaded = sem("grow_loaded")
        x_loaded = sem("x_loaded")
        act_chain = sem("act_chain")
        dve_chain = sem("dve_chain")
        h_ready = sem("h_ready")
        ssq_done = sem("ssq_done")
        var_done = sem("var_done")
        sd_done = sem("sd_done")
        rows_done = sem("rows_done")
        tr_done = sem("tr_done")
        in_hi = sem("in_hi")
        in_lo = sem("in_lo")
        half_done = sem("half_done")
        gate_done = sem("gate_done")
        pool_done = sem("pool_done")
        ax_read = sem("ax_read")
        sx_read = sem("sx_read")
        sb_read = sem("sb_read")
        pl_read = sem("pl_read")
        par_act = sem("par_act")
        par_dve = sem("par_dve")
        e_ready = sem("e_ready")
        ln_ready = sem("ln_ready")
        qf_ready = sem("qf_ready")
        k_ready = sem("k_ready")
        ex_ready = sem("ex_ready")
        exp_done = sem("exp_done")
        xs_ready = sem("xs_ready")
        level_done = sem("level_done")
        level_read = sem("level_read")
        v_ready = sem("v_ready")
        og_ready = sem("og_ready")
        ag_ready = sem("ag_ready")
        xin_ready = sem("xin_ready")
        gates_ready = sem("gates_ready")
        ta_ready = sem("ta_ready")
        m2_ready = sem("m2_ready")
        mult_ready = sem("mult_ready")
        sc_ready = sem("sc_ready")
        pd_ready = sem("pd_ready")
        gl_ready = sem("gl_ready")
        eg_done = sem("eg_done")
        kl_ready = sem("kl_ready")
        klt_done = sem("klt_done")
        klt_ready = sem("klt_ready")
        ds_done = sem("ds_done")
        st_ready = sem("st_ready")
        o_done = sem("o_done")
        osq_done = sem("osq_done")
        ovar_done = sem("ovar_done")
        osd_done = sem("osd_done")
        on_ready = sem("on_ready")
        ybt_done = sem("ybt_done")
        y_ready = sem("y_ready")
        y_hi = sem("y_hi")
        y_lo = sem("y_lo")
        out_done = sem("out_done")
        gu_done = sem("gu_done")
        s_ready = sem("s_ready")
        hid_ready = sem("hid_ready")
        hid_lo_ready = sem("hid_lo_ready")
        hid_hi_sem = sem("hid_hi_done")
        down_done = sem("down_done")
        down_added = sem("down_added")
        hn_stored = [sem(f"hn_stored{i}") for i in range(2)]
        moe_const_loaded = sem("moe_const_loaded")
        logits_done = sem("logits_done")
        route_ready = sem("route_ready")
        rank_done = sem("rank_done")
        slots_ready = sem("slots_ready")
        items_ready = sem("items_ready")
        idx_zeroed = sem("idx_zeroed")
        scattered = sem("scattered")
        idx_loaded = sem("idx_loaded")
        col_ready = sem("col_ready")
        xg_loaded = [sem(f"xg_loaded{i}") for i in range(2)]
        xt_tr = sem("xt_tr")
        xt_hi_done = sem("xt_hi_done")
        xt_lo_done = sem("xt_lo_done")
        g_done = sem("g_done")
        u_done = sem("u_done")
        se_ready = [sem(f"se_ready{i}") for i in range(2)]
        he_ready = [sem(f"he_ready{i}") for i in range(2)]
        t_done = [sem(f"t_done{i}") for i in range(2)]
        ht_hi_done = [sem(f"ht_hi_done{i}") for i in range(2)]
        ht_lo_done = [sem(f"ht_lo_done{i}") for i in range(2)]
        ye_done = sem("ye_done")
        ye_added = sem("ye_added")
        yacc_zeroed = sem("yacc_zeroed")
        y_stored = sem("y_stored")
        yacc_free = sem("yacc_free")
        mult_zeroed = sem("mult_zeroed")
        y_zeroed = sem("y_zeroed")
        comb_loaded = [sem(f"comb_loaded{i}") for i in range(8)]
        out_rows = sem("out_rows")
        out_stored = [sem(f"out_stored{i}") for i in range(2)]

        read_done = {FG: e_ready, Q: qf_ready, V: v_ready, A_X: ax_read, O_G: og_ready, A_G: ag_ready,
                     "gate": gates_ready, SC: sc_ready, SX: sx_read, SB: sb_read, PL: pl_read}

        def f32(ap):
            return ap.bitcast(F32)

        def pcol(name, i):
            return par[:, COLS[name] + i:COLS[name] + i + 1]

        def bank_of(key):
            return RING.index(key) % 4

        def output_done(eng, layer, key):
            s, u = key
            if s == "gate":
                eng.wait_ge(gate_done, 4 * layer + u + 1)
            elif s == "pool":
                eng.wait_ge(pool_done, 2 * layer + u + 1)
            elif u == 0:
                eng.wait_ge(half_done, N_IN * layer + ORDER.index(s) + 1)
            else:
                eng.wait_ge(w_used, layer * LAYER1 + ORDER.index(s) + 1)

        def bank_taken_over(eng, layer, key):
            n = RING.index(key) - 4
            if n >= 0:
                s, u = RING[n]
                eng.wait_ge(read_done[s], (4 if s == "gate" else 2) * layer + u + 1)

        def slice_of(dram, n, width=GW):
            return dram[:, n * width:(n + 1) * width].rearrange("(k p) n -> p k n", p=P)

        def raw3(slot, k=KT):
            return raw[:, slot, :].rearrange("p (k n) -> p k n", k=k)

        block = ctx.enter_context(nc.Block())

        @block.sync
        def _(sp):
            sp.dma_start(h[:, :, :], x[0].rearrange("(i p) d -> p i d", p=P)).then_inc(x_loaded, 16)

            def load(n, src, k=KT):
                if n >= 3:
                    sp.wait_ge(w_lo_done, n - 2)
                sp.dma_start(raw3(n % 3, k), src).then_inc(raw_loaded[n % 3], 16)

            for layer in range(DEPTH):
                first = layer * LAYER1
                for i, s in enumerate(ORDER):
                    load(first + i, slice_of(w_in[layer], s))
                for j in range(N_OUT):
                    load(first + N_IN + j, slice_of(w_out[layer], j))
                if layer == 0:
                    with sp.Fori(0, DC) as c:
                        for j in range(3):
                            n = DENSE0 + j
                            sp.wait_ge(w_lo_done, c * 3 + (n - 2))
                            if j < 2:
                                src = (w_gate, w_up)[j][0][:, bass.ds(c * GW, GW)] \
                                    .rearrange("(k p) n -> p k n", p=P)
                                dst = raw3(n % 3)
                            else:
                                src = w_down[0][bass.ds(c * GW, GW), :] \
                                    .rearrange("(k p) n -> p k n", p=P)
                                dst = raw3(n % 3, 2)
                            sp.dma_start(dst, src).then_inc(raw_loaded[n % 3], 16)

            sp.wait_ge(items_ready, 1)
            n_items = sp.value_load(items[0:1, 32:33], min_val=1, max_val=MAX_ITEMS)
            with sp.Fori(0, n_items) as n:
                e = sp.value_load(items[0:1, bass.ds(n, 1)], min_val=0, max_val=NE - 1)
                with sp.Fori(0, EC) as c:
                    for j in range(6):
                        sp.wait_ge(w_lo_done, (n * EC + c) * 6 + (MOE0 + j - 2))
                        slot = (MOE0 + j) % 3
                        if j < 4:
                            a = j // 2
                            src = (w1, w3)[j % 2][0][bass.ds(e, 1), a * 512:(a + 1) * 512, bass.ds(c * CW, CW)] \
                                .rearrange("x (k p) n -> p (x k) n", p=P)
                            dst = raw3(slot, 4)
                        else:
                            src = w2[0][bass.ds(e, 1), bass.ds(c * CW + (j - 4) * GW, GW), :] \
                                .rearrange("x (k p) n -> p (x k) n", p=P)
                            dst = raw3(slot, 2)
                        sp.dma_start(dst, src).then_inc(raw_loaded[slot], 16)
            for j in range(6):
                sp.wait_ge(w_lo_done, n_items * (EC * 6) + (MOE0 + j - 2))
                sp.sem_inc(raw_loaded[(MOE0 + j) % 3], 16)

            for i in range(NT):
                sp.wait_ge(out_rows, i + 1)
                sp.dma_start(out[0, i * P:(i + 1) * P, :], yacc[:, i % 2, :]).then_inc(out_stored[i % 2], 16)
            for i in range(2):
                sp.wait_ge(out_stored[i], 32)

        @block.gpsimd
        def _(pool):
            pool.dma_start(par[:, :], params[0]).then_inc(par_loaded, 16)
            pool.dma_start(grow, norm_rows[0].partition_broadcast(P)).then_inc(grow_loaded, 16)
            pool.dma_start(idt[:, :], ident).then_inc(const_loaded, 16)
            pool.dma_start(igate.rearrange("p c (l t) -> p (c l) t", t=P), masks).then_inc(masks_loaded, 16)
            pool.wait_ge(masks_loaded, 16)
            pool.tensor_copy(mask[:, :, :], igate.rearrange("p c (l t) -> p (c l) t", t=P)) \
                .then_inc(mask_ready, 1)
            pool.dma_start(idx_dram, zeros).then_inc(idx_zeroed, 16)
            pool.memset(mult[:, :, :], 0.0).then_inc(mult_zeroed, 1)
            pool.wait_ge(mult_zeroed, 1)
            rest = MAX_ITEMS - MIN_ITEMS
            pool.dma_start(y_dram[MIN_ITEMS * ROWS:, :].rearrange("(m p) d -> p m d", p=P),
                           mult.rearrange("p c t -> p (c t)").unsqueeze(1).broadcast_to([P, 2 * rest, D])) \
                .then_inc(y_zeroed, 16)
            pool.wait_ge(ds_done, 1)
            pool.dma_start(grow, norm_rows[1].partition_broadcast(P)).then_inc(grow_loaded, 16)
            pool.wait_ge(w_used, DENSE0)
            pool.dma_start(par[:, :], params[1]).then_inc(par_loaded, 16)
            pool.wait_ge(rows_done, 8)
            pool.dma_start(grow, norm_rows[2].partition_broadcast(P)).then_inc(grow_loaded, 16)
            pool.wait_ge(ds_done, 2)
            pool.dma_start(grow, norm_rows[3].partition_broadcast(P)).then_inc(grow_loaded, 16)
            pool.wait_ge(w_used, MOE0)
            pool.dma_start(mcon[:, :], moe_const).then_inc(moe_const_loaded, 16)
            pool.dma_start(wr[:, :, :], w_router[0].rearrange("(k p) e -> p k e", p=P)) \
                .then_inc(moe_const_loaded, 16)
            pool.dma_start(growf[:, :], norm_rows[4].partition_broadcast(P)).then_inc(moe_const_loaded, 16)
            for i in range(NT):
                pool.wait_ge(rows_done, 12 + i + 1)
                pool.dma_start(hn_dram[i * P:(i + 1) * P, :], rows[i % 2]).then_inc(hn_stored[i % 2], 16)

            pool.wait_ge(slots_ready, 1)
            pool.wait_ge(idx_zeroed, 16)
            for i in range(NT):
                for j in range(2):
                    if i + j:
                        pool.wait_ge(scattered, 16 * (2 * i + j))
                    pool.nop()
                    pool.indirect_dma_start(
                        idx_dram, bass.IndirectOffsetOnAxis(ap=slots[:, i, j:j + 1], axis=0),
                        tokens[:, i:i + 1], None).then_inc(scattered, 16)
            pool.wait_ge(scattered, 16 * 2 * NT)
            pool.dma_start(idx[:, :], idx_dram.rearrange("(m p) o -> p (m o)", p=P),
                           allow_slow_non_contiguous=True).then_inc(idx_loaded, 16)
            pool.wait_ge(idx_loaded, 16)
            for i in range(2):
                pool.wait_ge(hn_stored[i], 32)

            def gather(n, b):
                pool.tensor_copy(col[:, b:b + 1], idx[:, bass.ds(n * 2 + b, 1)]).then_inc(col_ready, 1)
                pool.wait_ge(col_ready, n * 2 + (b + 1))
                pool.nop(nofuse=True)
                pool.indirect_dma_start(xg[b][:, :], None, hn_dram,
                                        bass.IndirectOffsetOnAxis(ap=col[:, b:b + 1], axis=0)) \
                    .then_inc(xg_loaded[b], 16)

            for b in range(2):
                pool.tensor_copy(col[:, b:b + 1], idx[:, b:b + 1]).then_inc(col_ready, 1)
                pool.wait_ge(col_ready, b + 1)
                pool.indirect_dma_start(xg[b][:, :], None, hn_dram,
                                        bass.IndirectOffsetOnAxis(ap=col[:, b:b + 1], axis=0)) \
                    .then_inc(xg_loaded[b], 16)
            pool.wait_ge(y_zeroed, 16)
            pool.sem_inc(yacc_free, 1)
            pool.wait_ge(items_ready, 1)
            n_items = pool.value_load(items[0:1, 32:33], min_val=1, max_val=MAX_ITEMS)
            with pool.Fori(0, n_items) as n:
                for b in range(2):
                    pool.wait_ge(xt_tr, n * 2 + (b + 1))
                    gather(n + 1, b)
                pool.wait_ge(ye_added, pool.value_load(items[0:1, bass.ds(n + 33, 1)], min_val=1,
                                                       max_val=4 * EC * MAX_ITEMS) + 1)
                pool.nop(nofuse=True)
                pool.dma_start(y_dram[bass.ds(n * ROWS, ROWS), :].rearrange("(b p) d -> p b d", p=P),
                               yacc[:, :, :]).then_inc(y_stored, 16)
                pool.wait_ge(y_stored, n * 16 + 16)
                pool.sem_inc(yacc_free, 1)
            pool.wait_ge(w_lo_done, n_items * (EC * 6) + (MOE0 + 6))
            for b in range(2):
                pool.wait_ge(xg_loaded[b], n_items * 16 + 16)
            pool.nop(nofuse=True)
            for i in range(NT):
                for j in range(2):
                    pool.indirect_dma_start(comb[2 * i + j][:, :], None, y_dram,
                                            bass.IndirectOffsetOnAxis(ap=slots[:, i, j:j + 1], axis=0)) \
                        .then_inc(comb_loaded[2 * i + j], 16)

        @block.tensor
        def _(pe):
            def mm3(o_, lhi, llo, rhi, rlo, start, stop):
                pe.matmul(o_, lhi, rhi, start=start, stop=False)
                pe.matmul(o_, lhi, rlo, start=False, stop=False)
                return pe.matmul(o_, llo, rhi, start=False, stop=stop)

            def whi(n, k=KT):
                return w_his[:, n % 3, :].rearrange("p (k n) -> p k n", k=k)

            def wlo(n, k=KT):
                return w_los[:, n % 3, :].rearrange("p (k n) -> p k n", k=k)

            def norm_transposes(m):
                for i in range(NT):
                    pe.wait_ge(rows_done, 4 * m + i + 1)
                    for k in range(KT):
                        last = pe.transpose(ps[:, k, i * P:(i + 1) * P], rows[i % 2][:, k * P:(k + 1) * P],
                                            idt[:, :])
                    last.then_inc(tr_done, 1)

            def project(layer, i):
                s, n = ORDER[i], layer * LAYER1 + i
                pe.wait_ge(w_lo_done, n + 1)
                for u in range(2):
                    bank = bank_of((s, u))
                    bank_taken_over(pe, layer, (s, u))
                    if s in (V, O_G):
                        for t in range(2):
                            tt = 2 * u + t
                            for k in range(KT):
                                last = mm3(ps[:, bank, t * GW:(t + 1) * GW],
                                           act_hi[:, k, tt * P:(tt + 1) * P], act_lo[:, k, tt * P:(tt + 1) * P],
                                           whi(n)[:, k, :], wlo(n)[:, k, :], k == 0, k == KT - 1)
                    else:
                        for k in range(KT):
                            if i == 0 and u == 0:
                                pe.wait_ge(in_lo, (2 * layer) * KT + k + 1)
                            last = mm3(ps[:, bank, :], whi(n)[:, k, u * P:(u + 1) * P],
                                       wlo(n)[:, k, u * P:(u + 1) * P], act_hi[:, k, :], act_lo[:, k, :],
                                       k == 0, k == KT - 1)
                    last.then_inc((half_done, w_used)[u], 1)

            def level(layer, lv):
                pe.wait_ge(xs_ready, layer * LEVELS + lv + 1)
                if lv == 0:
                    pe.wait_ge(qf_ready, 2 * layer + 2)
                for hd in range(NH):
                    lo = HD * (hd % 2)
                    if lv:
                        pe.wait_ge(level_read, 4 * (layer * LEVELS + lv - 1) + hd + 1)
                    for c in range(NT):
                        if lv:
                            a = b = xs[lv % 2][lo:lo + HD, hd // 2, c * P:(c + 1) * P]
                        else:
                            a = keys[lo:lo + HD, hd // 2, c * P:(c + 1) * P]
                            b = qf[lo:lo + HD, hd // 2, c * P:(c + 1) * P]
                        last = pe.matmul(ps[:, 4 + hd, c * P:(c + 1) * P], a, b, start=True, stop=True)
                    last.then_inc(level_done, 1)

            def gates(layer):
                pe.wait_ge(xin_ready, layer + 1)
                for u in range(4):
                    bank = bank_of(("gate", u))
                    bank_taken_over(pe, layer, ("gate", u))
                    c0 = COLS[("bd_a", "bd_x")[u // 2]] + (u % 2) * P
                    pe.matmul(ps[:, bank, :], par[:, c0:c0 + P], x_in[:, u % 2, :], start=True, stop=True) \
                        .then_inc(gate_done, 1)

            def pool_product(layer):
                pe.wait_ge(pd_ready, layer + 1)
                for u in range(2):
                    bank = bank_of(("pool", u))
                    bank_taken_over(pe, layer, ("pool", u))
                    c0 = COLS["bd_p"] + u * P
                    pe.matmul(ps[:, bank, :], par[:, c0:c0 + P], igate[:, u, :], start=True, stop=True) \
                        .then_inc(pool_done, 1)

            def hgrn_tail(layer):
                pe.wait_ge(kl_ready, layer + 1)
                pe.wait_ge(level_read, 4 * LEVELS * (layer + 1))
                for c in range(NT - 1):
                    for ct in range(CT):
                        last = pe.transpose(ps[:, 4 + c // 2, (c % 2) * GW + ct * P:(c % 2) * GW + (ct + 1) * P],
                                            ex[1][:, ct, c * P:(c + 1) * P], idt[:, :])
                last.then_inc(klt_done, 1)
                pe.wait_ge(klt_ready, layer + 1)
                pe.wait_ge(v_ready, 2 * layer + 2)
                klt = xs[0].rearrange("p c t -> p (c t)").rearrange("p (n g) -> p n g", g=GW)
                for c in range(NT - 1):
                    for hd in range(NH):
                        lo = HD * (hd % 2)
                        last = pe.matmul(ps[lo:lo + HD, 6, c * P + (hd // 2) * HD:c * P + (hd // 2 + 1) * HD],
                                         klt[:, c, hd * HD:(hd + 1) * HD], vals[:, c, hd * HD:(hd + 1) * HD],
                                         start=True, stop=True)
                last.then_inc(ds_done, 1)
                for c in range(NT):
                    if c:
                        pe.wait_ge(st_ready, (NT - 1) * layer + c)
                    for hd in range(NH):
                        lo, ct = HD * (hd % 2), hd // 2
                        o_ = ps[:, (7, 4)[hd % 2], c * P + ct * HD:c * P + (ct + 1) * HD]
                        last = pe.matmul(o_, scores[:, hd, c, :], vals[:, c, hd * HD:(hd + 1) * HD],
                                         start=True, stop=c == 0)
                        if c:
                            last = pe.matmul(o_, ex[0][lo:lo + HD, ct, c * P:(c + 1) * P],
                                             state[lo:lo + HD, c, ct, :], start=False, stop=True)
                last.then_inc(o_done, 1)
                pool_product(layer)
                pe.wait_ge(on_ready, layer + 1)
                on = xs[1].rearrange("p c t -> p (c t)").rearrange("p (n g) -> p n g", g=GW)
                for ct in range(CT):
                    for c in range(NT):
                        last = pe.transpose(ps[:, 5 + ct, c * P:(c + 1) * P], on[:, c, ct * P:(ct + 1) * P],
                                            idt[:, :])
                last.then_inc(ybt_done, 1)

            def output(layer):
                pe.wait_ge(y_lo, 4 * (layer + 1))
                for j in range(N_OUT):
                    n = layer * LAYER1 + N_IN + j
                    pe.wait_ge(w_lo_done, n + 1)
                    for tt in range(NT):
                        for k in range(KT):
                            last = mm3(ps[:, 2 * tt + j // 2, (j % 2) * GW:(j % 2 + 1) * GW],
                                       act_hi[:, k, tt * P:(tt + 1) * P], act_lo[:, k, tt * P:(tt + 1) * P],
                                       whi(n)[:, k, :], wlo(n)[:, k, :], k == 0, k == KT - 1)
                        last.then_inc(w_used if tt == NT - 1 else out_done, 1)

            def dense_chunk(c):
                for j in range(2):
                    n = DENSE0 + j
                    pe.wait_ge(w_lo_done, c * 3 + (n + 1))
                    for ft in range(2):
                        for k in range(KT):
                            last = mm3(ps[:, 2 * j + ft, :], whi(n)[:, k, ft * P:(ft + 1) * P],
                                       wlo(n)[:, k, ft * P:(ft + 1) * P], act_hi[:, k, :], act_lo[:, k, :],
                                       k == 0, k == KT - 1)
                        last.then_inc((gu_done, w_used)[ft], 1)
                n = DENSE0 + 2
                pe.wait_ge(w_lo_done, c * 3 + (n + 1))
                for pair in range(2):
                    for ft in range(2):
                        if pair == 0:
                            pe.wait_ge(hid_lo_ready, c * 2 + (ft + 1))
                        for t in range(2):
                            tt = 2 * pair + t
                            if ft == 0:
                                pe.wait_ge(down_added, c * 4 + (tt + 3))
                            for half in range(2):
                                last = mm3(ps[:, 4 + 2 * t + half, :], hid_hi[:, ft, tt * P:(tt + 1) * P],
                                           hid_lo[:, ft, tt * P:(tt + 1) * P],
                                           whi(n, 2)[:, ft, half * 512:(half + 1) * 512],
                                           wlo(n, 2)[:, ft, half * 512:(half + 1) * 512], ft == 0, ft == 1)
                            if ft == 1:
                                last.then_inc(w_used if tt == NT - 1 else down_done, 1)

            pe.wait_ge(const_loaded, 16)
            for layer in range(DEPTH):
                norm_transposes(2 * layer)
                for i in range(N_IN):
                    project(layer, i)
                    if i >= 2:
                        level(layer, i - 2)
                    if i == 5:
                        gates(layer)
                hgrn_tail(layer)
                output(layer)
                norm_transposes(2 * layer + 1)
                if layer == 0:
                    pe.wait_ge(in_lo, 2 * KT)
                    with pe.Fori(0, DC) as c:
                        dense_chunk(c)

            pe.wait_ge(in_lo, 4 * KT)
            pe.wait_ge(moe_const_loaded, 48)
            for tt in range(NT):
                for k in range(KT):
                    for m, part in enumerate((act_hi, act_lo)):
                        last = pe.matmul(ps[:, 0, tt * NE:(tt + 1) * NE], f32(part[:, k, tt * P:(tt + 1) * P]),
                                         wr[:, k, :], start=(k == 0 and m == 0), stop=(k == KT - 1 and m == 1))
            last.then_inc(logits_done, 1)
            pe.wait_ge(route_ready, 1)
            chosen = rt[:, 8, :].rearrange("p (t e) -> p t e", e=NE)
            for tt in range(NT):
                for j in range(tt + 1):
                    c0 = MC_LOWER if j == tt else MC_ONES
                    pe.matmul(ps[:, 1, tt * NE:(tt + 1) * NE], mcon[:, c0:c0 + P], chosen[:, j, :],
                              start=j == 0, stop=j == tt)
            for j in range(NT):
                last = pe.matmul(ps[:, 2, 0:NE], mcon[:, MC_ONES:MC_ONES + P], chosen[:, j, :],
                                 start=j == 0, stop=j == NT - 1)
            last.then_inc(rank_done, 1)

            slot_hi = [w_his[:, (MOE0 + j) % 3, :] for j in range(3)] + [w_hi2[:, j, :] for j in range(3)]
            slot_lo = [w_los[:, (MOE0 + j) % 3, :] for j in range(3)] + [w_lo2[:, j, :] for j in range(3)]

            def up(b, j, q, release):
                pe.wait_ge(w_lo_done, q * 6 + (MOE0 + j + 1))
                a, which = j // 2, j % 2
                hi_ = slot_hi[j].rearrange("p (k n) -> p k n", k=4)
                lo_ = slot_lo[j].rearrange("p (k n) -> p k n", k=4)
                for k in range(4):
                    last = mm3(ps[:, 2 * b + which, :], xt_hi[:, b, 4 * a + k, :], xt_lo[:, b, 4 * a + k, :],
                               hi_[:, k, :], lo_[:, k, :], a == 0 and k == 0, a == 1 and k == 3)
                if release:
                    last.then_inc(w_used, 1)
                elif a == 1:
                    last.then_inc((g_done, u_done)[which], 1)

            def turn(b, count):
                pe.wait_ge(he_ready[b], count + 1)
                for f in range(4):
                    last = pe.transpose(ps[:, 4, f * P:(f + 1) * P], hid_e[:, b, f * P:(f + 1) * P], idt[:, :])
                last.then_inc(t_done[b], 1)

            def down(b, half, count, q, release):
                bank = ((5, 6), (7, 5))[b][half]
                if half == 0:
                    pe.wait_ge(ht_lo_done[b], count + 1)
                for f in range(4):
                    if f % 2 == 0 and half == 0:
                        pe.wait_ge(w_lo_done, q * 6 + (MOE0 + 5 + f // 2))
                    hi_ = slot_hi[4 + f // 2].rearrange("p (k n) -> p k n", k=2)
                    lo_ = slot_lo[4 + f // 2].rearrange("p (k n) -> p k n", k=2)
                    last = mm3(ps[:, bank, :], ht_hi[:, b, f, :], ht_lo[:, b, f, :],
                               hi_[:, f % 2, half * 512:(half + 1) * 512],
                               lo_[:, f % 2, half * 512:(half + 1) * 512], f == 0, f == 3)
                if release and half == 1:
                    last.then_inc(w_used, 2)
                else:
                    last.then_inc(ye_done, 1)

            pe.wait_ge(items_ready, 1)
            n_items = pe.value_load(items[0:1, 32:33], min_val=1, max_val=MAX_ITEMS)
            pairs = pe.alloc_register("pe_pairs")
            pe.reg_mov(pairs, 0)
            with pe.Fori(0, n_items) as n:
                for b in range(2):
                    pe.wait_ge(xg_loaded[b], n * 16 + 16)
                    for k in range(KT):
                        last = pe.transpose(ps[:, 2 * b + k // 4, (k % 4) * P:(k % 4 + 1) * P],
                                            xg[b][:, k * P:(k + 1) * P], idt[:, :])
                    last.then_inc(xt_tr, 1)
                pe.wait_ge(xt_lo_done, n * 2 + 2)
                two = pe.value_load(items[0:1, bass.ds(n + 16, 1)], min_val=0, max_val=1)
                with pe.Fori(0, EC) as c:
                    q = n * EC + c
                    v = pe.snap(pairs, min_val=0, max_val=EC * MAX_ITEMS)
                    with pe.If(two > 0):
                        for j in range(4):
                            up(0, j, q, False)
                        up(1, 0, q, True)
                        up(1, 1, q, True)
                        turn(0, q)
                        up(1, 2, q, True)
                        up(1, 3, q, True)
                        pe.wait_ge(ye_added, (q + v) * 2 + 1)
                        down(0, 0, q, q, False)
                        turn(1, v)
                        down(0, 1, q, q, False)
                        down(1, 0, v, q, False)
                        pe.wait_ge(ye_added, (q + v) * 2 + 2)
                        down(1, 1, v, q, True)
                        pe.reg_add(pairs, pairs, 1)
                    with pe.Else():
                        for j in range(4):
                            up(0, j, q, True)
                        turn(0, q)
                        pe.wait_ge(ye_added, (q + v) * 2 + 1)
                        down(0, 0, q, q, False)
                        down(0, 1, q, q, True)

        @block.scalar
        def _(act):
            chain = [0]

            def link(ins):
                chain[0] += 1
                ins.then_inc(act_chain, 1)
                act.wait_ge(act_chain, chain[0])

            def round_piece(n):
                act.wait_ge(raw_loaded[n % 3], 16 * (n // 3 + 1))
                if n >= 3:
                    act.wait_ge(w_used, n - 2)
                act.activation(w_his[:, n % 3, :], raw[:, n % 3, :], ACT.Copy).then_inc(w_hi_done, 1)

            def norm(m):
                for i in range(NT):
                    if m == 0:
                        act.wait_ge(x_loaded, 16)
                    else:
                        act.wait_ge(h_ready, 4 * (m - 1) + i + 1)
                    if i:
                        link(prev)
                    junk = xs[1] if m < 4 else silu_e
                    prev = act.activation(junk.rearrange("p c t -> p (c t)"), h[:, i, :], ACT.Square, accum_out=ssq[:, i:i + 1])
                prev.then_inc(ssq_done, 1)
                act.wait_ge(var_done, m + 1)
                act.activation(var, var, ACT.Sqrt).then_inc(sd_done, 1)

            def norm_evac(m):
                act.wait_ge(tr_done, 4 * (m + 1))
                for k in range(KT):
                    act.activation(act_hi[:, k, :], ps[:, k, :], ACT.Copy).then_inc(in_hi, 1)

            def from_ring(layer, key, dst, func, **kw):
                output_done(act, layer, key)
                return act.activation(dst, ps[:, bank_of(key), :], func, **kw)

            def level_exp(layer, lv):
                act.wait_ge(ex_ready, 7 * layer + lv)
                e = ex[lv % 2]
                act.activation(e[:, :, :], e[:, :, :], ACT.Exp).then_inc(exp_done, 1)

            def mixers(layer):
                first = layer * LAYER1
                norm(2 * layer)
                norm_evac(2 * layer)
                act.wait_ge(par_dve, 2 * layer + 1)
                act.activation(tmp[:, 0:6], tmp[:, 0:6], ACT.Exp).then_inc(par_act, 1)
                act.wait_ge(par_dve, 2 * layer + 2)
                act.wait_ge(e_ready, 2 * layer + 2)
                act.activation(keys[:, :, :], xs[1][:, :, :], ACT.Sigmoid).then_inc(ln_ready, 1)
                link(act.activation(xs[1][:, :, :], xs[1][:, :, :], ACT.Exp))
                for ct in range(CT):
                    act.activation(ex[0][:, ct, :], xs[1][:, ct, :], ACT.Ln, bias=1.0, scale=lbs[:, ct:ct + 1])
                act.activation(ex[1][:, :, :], xs[1][:, :, :], ACT.Ln, bias=1.0).then_inc(ln_ready, 1)
                for i in range(1, N_IN):
                    round_piece(first + i + 2)
                    if i < LEVELS:
                        level_exp(layer, i)
                    if i == 6:
                        for u in range(4):
                            dst = (r_gate, igate)[u // 2][:, u % 2, :]
                            ins = from_ring(layer, ("gate", u), dst, ACT.Sigmoid,
                                            bias=pcol(("b_a", "b_x")[u // 2], u % 2))
                            ins.then_inc(gates_ready, 1)
                        act.wait_ge(gates_ready, 4 * (layer + 1))
                        for ct in range(CT):
                            act.activation(tanh_l[:, ct, :], r_gate[:, ct, :], ACT.Tanh, scale=coef[:, ct:ct + 1]) \
                                .then_inc(ta_ready, 1)
                        for ct in range(CT):
                            act.activation(r_gate[:, ct, :], r_gate[:, ct, :], ACT.Exp, scale=coef[:, ct:ct + 1]) \
                                .then_inc(ta_ready, 1)
                    if i == 8:
                        act.wait_ge(m2_ready, layer + 1)
                        act.activation(mult[:, :, :], mult[:, :, :], ACT.Sqrt, scale=-1.0).then_inc(mult_ready, 1)
                    if i == 9:
                        act.wait_ge(gl_ready, layer + 1)
                        act.activation(ex[0][:, :, :], decay[:, :, :], ACT.Exp).then_inc(eg_done, 1)
                        act.activation(ex[1][:, :, :], ex[1][:, :, :], ACT.Exp).then_inc(eg_done, 1)
                    s = ORDER[i]
                    if s in (Q, V, O_G, A_G, SC):
                        dst, func, done = {
                            Q: (lambda u: qf[:, u, :], ACT.Silu, qf_ready),
                            V: (lambda u: vals[:, 2 * u:2 * u + 2, :].rearrange("p t g -> p (t g)"), ACT.Copy, v_ready),
                            O_G: (lambda u: ogate[:, 2 * u:2 * u + 2, :].rearrange("p t g -> p (t g)"), ACT.Silu, og_ready),
                            A_G: (lambda u: agate[:, u, :], ACT.Gelu_apprx_tanh, ag_ready),
                            SC: (lambda u: scv[:, u, :], ACT.Copy, sc_ready),
                        }[s]
                        for u in range(2):
                            from_ring(layer, (s, u), dst(u), func).then_inc(done, 1)
                round_piece(first + N_IN + 2)
                act.wait_ge(klt_done, layer + 1)
                xflat = xs[0].rearrange("p c t -> p (c t)")
                link(act.activation(xflat[:, 0:512], ps[:, 4, :], ACT.Copy))
                act.activation(xflat[:, 512:768], ps[:, 5, 0:256], ACT.Copy).then_inc(klt_ready, 1)
                act.wait_ge(o_done, layer + 1)
                sq = ex[1].rearrange("p c t -> p (c t)")
                act.activation(sq[:, 0:512], ps[:, 7, :], ACT.Square).then_inc(osq_done, 1)
                act.activation(sq[:, 512:1024], ps[:, 4, :], ACT.Square).then_inc(osq_done, 1)
                act.wait_ge(ovar_done, layer + 1)
                act.activation(o_var, o_var, ACT.Sqrt).then_inc(osd_done, 1)
                act.wait_ge(w_used, first + N_IN)
                for r, (k, src) in enumerate(((6, scv), (0, mult), (4, agate))):
                    act.wait_ge(y_ready, 3 * layer + r + 1)
                    act.activation(act_hi[:, k:k + 2, :], src[:, :, :], ACT.Copy).then_inc(y_hi, 1)
                act.wait_ge(ybt_done, layer + 1)
                act.activation(act_hi[:, 2:4, :], ps[:, 5:7, :], ACT.Copy).then_inc(y_hi, 1)
                if layer == 0:
                    for j in range(1, 5):
                        round_piece(first + N_IN + j + 2)
                else:
                    round_piece(first + N_IN + 3)

            for n in range(3):
                round_piece(n)
            mixers(0)
            norm(1)
            norm_evac(1)
            with act.Fori(0, DC) as c:
                for ft in range(2):
                    if ft == 0:
                        act.wait_ge(gu_done, c * 2 + 1)
                    else:
                        act.wait_ge(w_used, c * 3 + (DENSE0 + 1))
                    act.activation(silu_d[:, ft, :], ps[:, ft, :], ACT.Silu).then_inc(s_ready, 1)

                def round_next(j):
                    n = DENSE0 + 3 + j
                    act.wait_ge(raw_loaded[n % 3], c * 16 + 16 * (n // 3 + 1))
                    act.wait_ge(w_used, c * 3 + (n - 2))
                    act.activation(w_his[:, n % 3, :], raw[:, n % 3, :], ACT.Copy).then_inc(w_hi_done, 1)

                round_next(0)
                for ft in range(2):
                    act.wait_ge(hid_ready, c * 2 + (ft + 1))
                    act.activation(hid_hi[:, ft, :], hid_d[:, ft, :], ACT.Copy).then_inc(hid_hi_sem, 1)
                round_next(1)
                round_next(2)
            mixers(1)
            norm(3)
            norm_evac(3)
            act.wait_ge(route_ready, 2)
            act.activation(rt[:, 9, 4:8], rt[:, 9, 4:8], ACT.Exp).then_inc(par_act, 1)

            slot_hi = [w_his[:, (MOE0 + j) % 3, :] for j in range(3)] + [w_hi2[:, j, :] for j in range(3)]

            def round_ahead(j, q1):
                n = MOE0 + j
                act.wait_ge(raw_loaded[n % 3], q1 * 32 + 16 * (n // 3 + 1))
                act.wait_ge(w_used, MOE0 if isinstance(q1, int) else q1 * 6 + (n - 5))
                act.activation(slot_hi[j], raw[:, n % 3, :], ACT.Copy).then_inc(w_hi_done, 1)

            def silu_block(b, q, v, early=False):
                if early:
                    act.wait_ge(g_done, v + 1)
                else:
                    act.wait_ge(w_used, q * 6 + (MOE0 + 3))
                act.activation(silu_e[:, b, :], ps[:, 2 * b, :], ACT.Silu).then_inc(se_ready[b], 1)

            def turned(b, count):
                act.wait_ge(t_done[b], count + 1)
                act.activation(ht_hi[:, b, :, :].rearrange("p f t -> p (f t)"), ps[:, 4, :], ACT.Copy) \
                    .then_inc(ht_hi_done[b], 1)

            act.wait_ge(items_ready, 1)
            for i in range(2):
                act.wait_ge(hn_stored[i], 32)
            for j in range(6):
                round_ahead(j, 0)
            n_items = act.value_load(items[0:1, 32:33], min_val=1, max_val=MAX_ITEMS)
            pairs = act.alloc_register("act_pairs")
            act.reg_mov(pairs, 0)
            with act.Fori(0, n_items) as n:
                for b in range(2):
                    act.wait_ge(xt_tr, n * 2 + (b + 1))
                    act.activation(xt_hi[:, b, :, :].rearrange("p k t -> p (k t)"),
                                   ps[:, 2 * b:2 * b + 2, :].rearrange("p a t -> p (a t)"), ACT.Copy) \
                        .then_inc(xt_hi_done, 1)
                two = act.value_load(items[0:1, bass.ds(n + 16, 1)], min_val=0, max_val=1)
                with act.Fori(0, EC) as c:
                    q = n * EC + c
                    v = act.snap(pairs, min_val=0, max_val=EC * MAX_ITEMS)
                    with act.If(two > 0):
                        silu_block(0, q, v, early=True)
                        round_ahead(0, q + 1)
                        round_ahead(1, q + 1)
                        turned(0, q)
                        round_ahead(2, q + 1)
                        silu_block(1, q, v)
                        round_ahead(3, q + 1)
                        turned(1, v)
                        round_ahead(4, q + 1)
                        round_ahead(5, q + 1)
                        act.reg_add(pairs, pairs, 1)
                    with act.Else():
                        round_ahead(0, q + 1)
                        round_ahead(1, q + 1)
                        silu_block(0, q, v)
                        round_ahead(2, q + 1)
                        turned(0, q)
                        round_ahead(3, q + 1)
                        round_ahead(4, q + 1)
                        round_ahead(5, q + 1)
            norm(4)

        @block.vector
        def _(dve):
            chain = [0]

            def link(ins):
                chain[0] += 1
                ins.then_inc(dve_chain, 1)
                dve.wait_ge(dve_chain, chain[0])

            def rest_piece(n):
                dve.wait_ge(w_hi_done, n + 1)
                dve.tensor_tensor(w_los[:, n % 3, :], raw[:, n % 3, :], f32(w_his[:, n % 3, :]), ALU.subtract) \
                    .then_inc(w_lo_done, 1)

            def norm(m, dst=None):
                dve.wait_ge(ssq_done, m + 1)
                dve.tensor_scalar(var, ssq, 1.0 / D, EPS, ALU.mult, ALU.add).then_inc(var_done, 1)
                dve.wait_ge(sd_done, m + 1)
                link(dve.reciprocal(rstd, var))
                if m < 4:
                    dve.wait_ge(grow_loaded, 16 * (m + 1))
                for i in range(NT):
                    if m < 4:
                        if i >= 2:
                            dve.wait_ge(tr_done, 4 * m + i - 1)
                            if m == 3:
                                dve.wait_ge(hn_stored[i % 2], 16)
                        dve.scalar_tensor_tensor(rows[i % 2], h[:, i, :], rstd[:, i:i + 1], grow,
                                                 ALU.mult, ALU.mult).then_inc(rows_done, 1)
                    else:
                        if i >= 2:
                            dve.wait_ge(out_stored[i % 2], 16)
                        dve.scalar_tensor_tensor(yacc[:, i % 2, :], h[:, i, :], rstd[:, i:i + 1], growf[:, :],
                                                 ALU.mult, ALU.mult).then_inc(out_rows, 1)

            def norm_evac(m):
                for k in range(KT):
                    dve.wait_ge(in_hi, m * KT + k + 1)
                    dve.tensor_tensor(act_lo[:, k, :], ps[:, k, :], f32(act_hi[:, k, :]), ALU.subtract) \
                        .then_inc(in_lo, 1)

            def ring_ps(layer, key):
                output_done(dve, layer, key)
                return ps[:, bank_of(key), :]

            def coefficients(layer):
                dve.wait_ge(par_loaded, 16 * (layer + 1))
                lam = par[:, COLS["lam"]:COLS["lam"] + 2]
                lb0 = par[:, COLS["hlb"]:COLS["hlb"] + 2]
                lb1 = par[:, COLS["hlb"] + 2:COLS["hlb"] + 4]
                link(dve.tensor_scalar(tmp[:, 6:8], lam, -1.0, None, ALU.mult))
                link(dve.tensor_tensor(tmp[:, 8:10], lb0, lb1, ALU.max))
                link(dve.tensor_tensor(tmp[:, 10:12], lam, tmp[:, 6:8], ALU.min))
                link(dve.tensor_copy(tmp[:, 0:2], tmp[:, 10:12]))
                link(dve.tensor_tensor(tmp[:, 2:4], lb0, tmp[:, 8:10], ALU.subtract))
                dve.tensor_tensor(tmp[:, 4:6], lb1, tmp[:, 8:10], ALU.subtract).then_inc(par_dve, 1)
                dve.wait_ge(par_act, layer + 1)
                y, z, z2, acc = tmp[:, 0:2], tmp[:, 8:10], tmp[:, 10:12], tmp[:, 12:14]
                link(dve.tensor_scalar(z, y, 2.0, None, ALU.add))
                link(dve.reciprocal(z2, z))
                link(dve.tensor_tensor(z, y, z2, ALU.mult))
                link(dve.tensor_tensor(z2, z, z, ALU.mult))
                link(dve.tensor_scalar(acc, z2, 1.0 / 17, 1.0 / 15, ALU.mult, ALU.add))
                for d in (13, 11, 9, 7, 5, 3, 1):
                    link(dve.tensor_tensor(acc, acc, z2, ALU.mult))
                    link(dve.tensor_scalar(acc, acc, 1.0 / d, None, ALU.add))
                link(dve.tensor_tensor(acc, acc, z, ALU.mult))
                link(dve.tensor_scalar(tmp[:, 14:16], tmp[:, 6:8], 0.0, -8.0, ALU.max, ALU.mult))
                link(dve.scalar_tensor_tensor(coef, acc, -16.0, tmp[:, 14:16], ALU.mult, ALU.add))
                e0, e1 = tmp[:, 2:4], tmp[:, 4:6]
                link(dve.tensor_tensor(tmp[:, 16:18], e0, e1, ALU.add))
                link(dve.reciprocal(tmp[:, 18:20], tmp[:, 16:18]))
                link(dve.tensor_tensor(e0, e0, tmp[:, 18:20], ALU.mult))
                link(dve.tensor_tensor(e1, e1, tmp[:, 18:20], ALU.mult))
                cum = e0
                if layer:
                    link(dve.tensor_tensor(tmp[:, 16:18], e0, e1, ALU.add))
                    cum = tmp[:, 16:18]
                link(dve.tensor_tensor(lbs, cum, e0, ALU.subtract))
                dve.tensor_scalar(omlb, lbs, -1.0, 1.0, ALU.mult, ALU.add).then_inc(par_dve, 1)
                dve.wait_ge(par_dve, 2 * layer + 2)

            def views(t, half):
                v = t.rearrange("p c t -> p (c t)").rearrange("p (n x h) -> p n x h", x=2, h=half)
                return v[:, :, 0, :], v[:, :, 1, :]

            def level_exponents(layer, lv):
                half = 1 << (lv - 1)
                left, right = views(decay, half)
                e_left, e_right = views(ex[lv % 2], half)
                mid = left[:, :, half - 1:half].broadcast_to([P, CT * T // (2 * half), half])
                dve.tensor_tensor(e_left, mid, left, ALU.subtract)
                dve.tensor_tensor(e_right, right, mid, ALU.subtract).then_inc(ex_ready, 1)

            def level_operand(layer, lv):
                half = 1 << (lv - 1)
                if lv >= 3:
                    dve.wait_ge(level_done, 4 * (layer * LEVELS + lv - 1))
                dve.wait_ge(exp_done, 7 * layer + lv)
                e_left, e_right = views(ex[lv % 2], half)
                x_left, x_right = views(xs[lv % 2], half)
                k_left, _ = views(keys, half)
                _, q_right = views(qf, half)
                dve.tensor_tensor(x_left, k_left, e_left, ALU.mult)
                dve.tensor_tensor(x_right, q_right, e_right, ALU.mult).then_inc(xs_ready, 1)

            def level_keep(layer, lv):
                if layer == 0 and lv == 0:
                    dve.wait_ge(mask_ready, 1)
                m = mask[:, lv, :].unsqueeze(1).broadcast_to([P, NT, P])
                for hd in range(NH):
                    dve.wait_ge(level_done, 4 * (layer * LEVELS + lv) + hd + 1)
                    dve.copy_predicated(scores[:, hd, :, :], m, ps[:, 4 + hd, :].rearrange("p (c t) -> p c t", c=NT)) \
                        .then_inc(level_read, 1)

            def lo_of(layer, k, src):
                dve.tensor_tensor(act_lo[:, k:k + 2, :], src, f32(act_hi[:, k:k + 2, :]), ALU.subtract) \
                    .then_inc(y_lo, 1)

            def mixers(layer):
                first = layer * LAYER1
                norm(2 * layer)
                norm_evac(2 * layer)
                coefficients(layer)
                for u in range(2):
                    src = ring_ps(layer, (FG, u))
                    ins = dve.tensor_scalar(xs[1][:, u, :], src, -1.0, 80.0, ALU.mult, ALU.min)
                    ins.then_inc(e_ready, 1)
                dve.memset(scores[:, :, :, :], 0.0).then_inc(dve_chain, 1)
                dve.memset(lru_in[:, :, 0:3], 0.0).then_inc(dve_chain, 1)
                dve.memset(sxv[:, :, 0:2], 0.0).then_inc(dve_chain, 1)
                chain[0] += 3
                dve.wait_ge(ln_ready, 2 * layer + 1)
                for ct in range(CT):
                    ins = dve.tensor_scalar(keys[:, ct, :], keys[:, ct, :], omlb[:, ct:ct + 1], None, ALU.mult)
                ins.then_inc(xs_ready, 1)
                dve.wait_ge(ln_ready, 2 * layer + 2)
                link(dve.tensor_tensor(xs[0][:, :, :], ex[0][:, :, :], ex[1][:, :, :], ALU.subtract))
                for ct in range(CT):
                    for c in range(NT):
                        lf = xs[0][:, ct, c * P:(c + 1) * P]
                        ins = dve.tensor_tensor_scan(decay[:, ct, c * P:(c + 1) * P], lf, lf, 0.0, ALU.add, ALU.min)
                link(ins)
                for i in range(1, N_IN):
                    rest_piece(first + i + 2)
                    if i < LEVELS:
                        if i >= 3:
                            dve.wait_ge(xs_ready, layer * LEVELS + i - 1)
                        level_exponents(layer, i)
                    if i == 2:
                        dve.wait_ge(qf_ready, 2 * layer + 2)
                    if 1 <= i - 1 < LEVELS:
                        level_operand(layer, i - 1)
                    if i >= 3:
                        level_keep(layer, i - 3)
                    if i == 4:
                        dve.wait_ge(dve_chain, chain[0])
                        for ct in range(CT):
                            link(dve.tensor_scalar(x_in[:, ct, :], lru_in[:, ct, 3:3 + T], pcol("conv_w", 6 + ct),
                                                   pcol("conv_b", ct), ALU.mult, ALU.add))
                            for j in (2, 1, 0):
                                ins = dve.scalar_tensor_tensor(
                                    x_in[:, ct, :], lru_in[:, ct, j:j + T], pcol("conv_w", 2 * j + ct),
                                    x_in[:, ct, :], ALU.mult, ALU.add)
                                if j or ct == 0:
                                    link(ins)
                        ins.then_inc(xin_ready, 1)
                    if i == 6:
                        dve.wait_ge(og_ready, 2 * layer + 2)
                        g = par[:, COLS["norm_g"]:COLS["norm_g"] + GW].unsqueeze(1).broadcast_to([P, NT, GW])
                        link(dve.tensor_tensor(ogate[:, :, :], ogate[:, :, :], g, ALU.mult))
                    if i == 8:
                        dve.wait_ge(y_zeroed, 16)
                        dve.wait_ge(ta_ready, 4 * (layer + 1))
                        link(dve.tensor_tensor(mult[:, :, :], r_gate, r_gate, ALU.mult))
                        dve.scalar_tensor_tensor(mult[:, :, :], mult[:, :, :], 1.0, tanh_l, ALU.add, ALU.mult) \
                            .then_inc(m2_ready, 1)
                        link(dve.tensor_tensor(igate[:, :, :], igate[:, :, :], x_in, ALU.mult))
                        for ct in range(CT):
                            link(dve.tensor_scalar(scv[:, ct, :], sxv[:, ct, 2:2 + T], pcol("sconv_w", 4 + ct),
                                                   None, ALU.mult))
                            for j in (1, 0):
                                link(dve.scalar_tensor_tensor(
                                    scv[:, ct, :], sxv[:, ct, j:j + T], pcol("sconv_w", 2 * j + ct),
                                    scv[:, ct, :], ALU.mult, ALU.add))
                        dve.wait_ge(mult_ready, layer + 1)
                        link(dve.tensor_tensor(igate[:, :, :], igate[:, :, :], mult[:, :, :], ALU.mult))
                        for ct in range(CT):
                            ins = dve.tensor_tensor_scan(mult[:, ct, :], r_gate[:, ct, :], igate[:, ct, :], 0.0,
                                                         ALU.mult, ALU.add)
                            link(ins)
                        dve.wait_ge(ag_ready, 2 * layer + 2)
                        link(dve.tensor_tensor(mult[:, :, :], mult[:, :, :], agate[:, :, :], ALU.mult))
                        link(dve.memset(lru_in[:, :, 0:16], 0.0))
                    if i == 9:
                        last = decay[:, :, :].rearrange("p c (n t) -> p (c n) t", t=P)
                        dve.tensor_tensor(ex[1].rearrange("p c (n t) -> p (c n) t", t=P),
                                          last[:, :, P - 1:P].broadcast_to([P, CT * NT, P]), last,
                                          ALU.subtract).then_inc(gl_ready, 1)
                    s = ORDER[i]
                    if s == A_X:
                        for u in range(2):
                            ins = dve.tensor_copy(lru_in[:, u, 3:3 + T], ring_ps(layer, (s, u)))
                            ins.then_inc(ax_read, 1)
                        dve.wait_ge(ax_read, 2 * (layer + 1))
                    elif s == SX:
                        dve.wait_ge(sc_ready, 2 * layer + 2)
                        for u in range(2):
                            ins = dve.tensor_tensor(sxv[:, u, 2:2 + T], ring_ps(layer, (s, u)), scv[:, u, :], ALU.mult)
                            ins.then_inc(sx_read, 1)
                        dve.wait_ge(sx_read, 2 * (layer + 1))
                    elif s == SB:
                        for u in range(2):
                            ins = dve.tensor_tensor(scv[:, u, :], ring_ps(layer, (s, u)), scv[:, u, :], ALU.mult)
                            ins.then_inc(sb_read, 1)
                        dve.wait_ge(sb_read, 2 * (layer + 1))
                        dve.sem_inc(y_ready, 1)
                        dve.sem_inc(y_ready, 1)
                    elif s == PL:
                        for u in range(2):
                            ins = dve.tensor_copy(lru_in[:, u, 16:16 + T], ring_ps(layer, (s, u)))
                            ins.then_inc(pl_read, 1)
                        dve.wait_ge(pl_read, 2 * (layer + 1))
                N = T + 16
                link(dve.tensor_tensor(w1b[:, :, 1:N], lru_in[:, :, 1:N], lru_in[:, :, 0:N - 1], ALU.add))
                link(dve.tensor_tensor(w2b[:, :, 3:N], w1b[:, :, 3:N], w1b[:, :, 1:N - 2], ALU.add))
                link(dve.tensor_tensor(w1b[:, 1, 7:N], w2b[:, 1, 7:N], w2b[:, 1, 3:N - 4], ALU.add))
                link(dve.tensor_tensor(w2b[:, 1, 15:N], w1b[:, 1, 15:N], w1b[:, 1, 7:N - 8], ALU.add))
                ramp = par[:, COLS["ramp"]:COLS["ramp"] + 32].rearrange("p (c t) -> p c t", c=2)
                for lo, w in ((0, w1b), (HD, w2b)):
                    link(dve.tensor_tensor(w[lo:lo + HD, :, 16:32], w[lo:lo + HD, :, 16:32], ramp[lo:lo + HD], ALU.mult))
                for ct in range(CT):
                    for lo, w in ((0, w1b), (HD, w2b)):
                        win = 2 << (2 * ct + lo // HD)
                        ins = dve.scalar_tensor_tensor(
                            igate[lo:lo + HD, ct, :], w[lo:lo + HD, ct, 16:N], 1.0 / win,
                            lru_in[lo:lo + HD, ct, 16:N], ALU.mult, ALU.subtract)
                        if (ct, lo) != (1, HD):
                            link(ins)
                ins.then_inc(pd_ready, 1)
                rest_piece(first + N_IN + 2)
                dve.wait_ge(eg_done, 2 * (layer + 1))
                link(dve.tensor_copy(eg_last, ex[0].rearrange("p c (n t) -> p c n t", t=P)[:, :, :, P - 1]))
                dve.tensor_tensor(ex[1][:, :, :], keys[:, :, :], ex[1][:, :, :], ALU.mult).then_inc(kl_ready, 1)
                link(dve.tensor_tensor(ex[0][:, :, :], qf[:, :, :], ex[0][:, :, :], ALU.mult))
                level_keep(layer, 7)
                dve.wait_ge(ds_done, layer + 1)
                for c in range(NT - 1):
                    for ct in range(CT):
                        d_s = ps[:, 6, c * P + ct * HD:c * P + (ct + 1) * HD]
                        if c == 0:
                            ins = dve.tensor_copy(state[:, 1, ct, :], d_s)
                        else:
                            ins = dve.scalar_tensor_tensor(state[:, c + 1, ct, :], state[:, c, ct, :],
                                                           eg_last[:, ct, c:c + 1], d_s, ALU.mult, ALU.add)
                    ins.then_inc(st_ready, 1)
                    dve.wait_ge(st_ready, (NT - 1) * layer + c + 1)
                for u in range(2):
                    ins = dve.tensor_scalar(agate[:, u, :], ring_ps(layer, ("pool", u)), pcol("pool_scale", u),
                                            None, ALU.mult)
                    if u == 0:
                        link(ins)
                ins.then_inc(y_ready, 1)
                dve.wait_ge(osq_done, 2 * (layer + 1))
                link(dve.tensor_reduce(o_ssq, ex[1].rearrange("p c t -> p (c t)").rearrange("p (n v) -> p n v", v=HD),
                                       AX.X, ALU.add))
                dve.tensor_scalar(o_var, o_ssq, 1.0 / HD, HEAD_EPS, ALU.mult, ALU.add).then_inc(ovar_done, 1)
                dve.wait_ge(osd_done, layer + 1)
                link(dve.reciprocal(o_rstd, o_var))
                on = xs[1].rearrange("p c t -> p (c t)")
                by_parity = on.rearrange("p (n b v) -> p n b v", b=2, v=HD)
                for half, bank in ((0, 7), (1, 4)):
                    link(dve.tensor_tensor(
                        by_parity[:, :, half, :],
                        ps[:, bank, :].rearrange("p (n v) -> p n v", v=HD),
                        o_rstd[:, half * 8:(half + 1) * 8].unsqueeze(2).broadcast_to([P, 8, HD]), ALU.mult))
                dve.tensor_tensor(on, on, ogate.rearrange("p n g -> p (n g)"), ALU.mult).then_inc(on_ready, 1)
                for r, (k, src) in enumerate(((6, scv), (0, mult), (4, agate))):
                    dve.wait_ge(y_hi, 4 * layer + r + 1)
                    lo_of(layer, k, src[:, :, :])
                dve.wait_ge(y_hi, 4 * layer + 4)
                lo_of(layer, 2, ps[:, 5:7, :])
                for j in range(1, 4):
                    if layer == 0 or j == 1:
                        rest_piece(first + N_IN + j + 2)
                    if j in (2, 3):
                        half = j - 2
                        for tt in range(NT):
                            if tt < NT - 1:
                                dve.wait_ge(out_done, 3 * (4 * layer + 2 * half + 1) + tt + 1)
                            else:
                                dve.wait_ge(w_used, first + N_IN + 2 * half + 2)
                            s_ = slice(half * 512, (half + 1) * 512)
                            ins = dve.tensor_tensor(h[:, tt, s_], h[:, tt, s_], ps[:, 2 * tt + half, :], ALU.add)
                            if half:
                                ins.then_inc(h_ready, 1)
                            else:
                                link(ins)
                if layer == 0:
                    rest_piece(first + N_IN + 6)

            for n in range(3):
                rest_piece(n)
            dve.wait_ge(x_loaded, 16)
            mixers(0)
            norm(1)
            norm_evac(1)
            dve.sem_inc(down_added, 4)
            with dve.Fori(0, DC) as c:
                def rest_next(j):
                    n = DENSE0 + 3 + j
                    dve.wait_ge(w_hi_done, c * 3 + (n + 1))
                    dve.tensor_tensor(w_los[:, n % 3, :], raw[:, n % 3, :], f32(w_his[:, n % 3, :]), ALU.subtract) \
                        .then_inc(w_lo_done, 1)

                for ft in range(2):
                    dve.wait_ge(s_ready, c * 2 + (ft + 1))
                    if ft == 0:
                        dve.wait_ge(gu_done, c * 2 + 2)
                    else:
                        dve.wait_ge(w_used, c * 3 + (DENSE0 + 2))
                    dve.tensor_tensor(hid_d[:, ft, :], silu_d[:, ft, :], ps[:, 2 + ft, :], ALU.mult) \
                        .then_inc(hid_ready, 1)
                    dve.wait_ge(hid_hi_sem, c * 2 + (ft + 1))
                    dve.tensor_tensor(hid_lo[:, ft, :], hid_d[:, ft, :], f32(hid_hi[:, ft, :]), ALU.subtract) \
                        .then_inc(hid_lo_ready, 1)
                rest_next(0)
                rest_next(1)
                for tt in range(NT):
                    if tt < NT - 1:
                        dve.wait_ge(down_done, c * 3 + (tt + 1))
                    else:
                        dve.wait_ge(w_used, c * 3 + (DENSE0 + 3))
                    b = 4 + 2 * (tt % 2)
                    dve.tensor_tensor(h[:, tt, :], h[:, tt, :], ps[:, b:b + 2, :].rearrange("p a d -> p (a d)"),
                                      ALU.add).then_inc(down_added, 1)
                rest_next(2)
            dve.wait_ge(down_added, 4 * DC + 4)
            dve.sem_inc(h_ready, 4)
            mixers(1)
            norm(3)
            norm_evac(3)

            dve.wait_ge(logits_done, 1)
            dve.wait_ge(moe_const_loaded, 48)

            def r3(i):
                return rt[:, i, :].rearrange("p (t e) -> p t e", e=NE)

            def wide(ap):
                return ap.unsqueeze(2).broadcast_to([P, NT, NE])

            def per_e(ap):
                return ap.unsqueeze(1).broadcast_to([P, NT, NE])

            LG, EQ, CAND, OH1, OH2, LG2, SLOT, PROD, CH, SM, RK, ST = range(12)
            iota8 = mcon[:, MC_IOTA:MC_IOTA + NE]
            m1, m2, first_e = rt[:, SM, 0:4], rt[:, SM, 4:8], rt[:, SM, 8:12]
            link(dve.tensor_copy(rt[:, LG, :], ps[:, 0, 0:NT * NE]))

            def choose(lg, best, oh):
                link(dve.tensor_reduce(best, r3(lg), AX.X, ALU.max))
                link(dve.tensor_tensor(r3(EQ), r3(lg), wide(best), ALU.is_equal))
                link(dve.tensor_tensor(r3(CAND), r3(EQ), per_e(iota8), ALU.mult))
                link(dve.tensor_reduce(first_e, r3(CAND), AX.X, ALU.min))
                link(dve.tensor_tensor(r3(oh), per_e(iota8), wide(first_e), ALU.is_equal))

            choose(LG, m1, OH1)
            link(dve.scalar_tensor_tensor(rt[:, LG2, :], rt[:, OH1, :], -1e30, rt[:, LG, :], ALU.mult, ALU.add))
            choose(LG2, m2, OH2)
            dve.tensor_tensor(rt[:, CH, :], rt[:, OH1, :], rt[:, OH2, :], ALU.add).then_inc(route_ready, 1)
            dve.tensor_tensor(rt[:, 9, 4:8], m2, m1, ALU.subtract).then_inc(route_ready, 1)
            dve.wait_ge(par_act, DEPTH + 1)
            g1, g2 = rt[:, 12, 0:4], rt[:, 12, 4:8]
            link(dve.tensor_scalar(rt[:, 12, 8:12], rt[:, 9, 4:8], 1.0, None, ALU.add))
            link(dve.reciprocal(g1, rt[:, 12, 8:12]))
            link(dve.tensor_tensor(g2, rt[:, 9, 4:8], g1, ALU.mult))
            dve.wait_ge(rank_done, 1)
            cnt, n_of, incl, start = (rt[:, 13, 8 * i:8 * i + 8] for i in range(4))
            has2 = rt[:, 14, 0:8]
            has1 = rt[:, 14, 8:16]
            link(dve.tensor_copy(rt[:, RK, :], ps[:, 1, 0:NT * NE]))
            link(dve.tensor_copy(cnt, ps[:, 2, 0:NE]))
            link(dve.tensor_scalar(has1, cnt, 0.0, None, ALU.is_gt))
            link(dve.tensor_scalar(has2, cnt, float(ROWS), None, ALU.is_gt))
            link(dve.tensor_tensor(n_of, has1, has2, ALU.add))
            link(dve.tensor_tensor_scan(incl, n_of, mcon[:, MC_ZERO:MC_ZERO + NE], 0.0, ALU.add, ALU.add))
            link(dve.tensor_tensor(start, incl, n_of, ALU.subtract))
            link(dve.tensor_scalar(rt[:, 15, 0:8], start, float(ROWS), None, ALU.mult))
            link(dve.tensor_tensor(r3(SLOT), r3(RK), per_e(rt[:, 15, 0:8]), ALU.add))
            for j, oh in enumerate((OH1, OH2)):
                link(dve.tensor_tensor(r3(PROD), r3(SLOT), r3(oh), ALU.mult))
                link(dve.tensor_reduce(rt[:, 16, 4 * j:4 * j + 4], r3(PROD), AX.X, ALU.add))
                link(dve.tensor_copy(slots[:, :, j], rt[:, 16, 4 * j:4 * j + 4]))
            dve.tensor_copy(tokens[:, :], mcon[:, MC_TOK:MC_TOK + NT]).then_inc(slots_ready, 1)
            w3v = [rtw[0:1, i, :].rearrange("p (n e) -> p n e", e=NE) for i in range(5)]

            def over_n(ap):
                return ap.unsqueeze(1).broadcast_to([1, 16, NE])

            n_row = mcon[0:1, MC_N:MC_N + 128].rearrange("p (n e) -> p n e", e=NE)
            e_row = mcon[0:1, MC_E:MC_E + NE]
            s1 = rt[0:1, 17, 0:8]
            over1, over2 = rt[0:1, 17, 8:16], rt[0:1, 17, 16:24]
            link(dve.tensor_scalar(s1, start[0:1], 1.0, None, ALU.add))
            link(dve.tensor_scalar(over1, cnt[0:1], float(P), None, ALU.is_gt))
            link(dve.tensor_scalar(over2, cnt[0:1], float(ROWS + P), None, ALU.is_gt))
            link(dve.tensor_tensor(w3v[0], n_row, over_n(start[0:1]), ALU.is_equal))
            link(dve.tensor_tensor(w3v[0], w3v[0], over_n(has1[0:1]), ALU.mult))
            link(dve.tensor_tensor(w3v[1], n_row, over_n(s1), ALU.is_equal))
            link(dve.tensor_tensor(w3v[1], w3v[1], over_n(has2[0:1]), ALU.mult))
            link(dve.tensor_tensor(w3v[2], w3v[0], w3v[1], ALU.add))
            link(dve.tensor_tensor(w3v[2], w3v[2], over_n(e_row), ALU.mult))
            link(dve.tensor_reduce(rt[0:1, 18, 0:16], w3v[2], AX.X, ALU.add))
            link(dve.tensor_tensor(w3v[0], w3v[0], over_n(over1), ALU.mult))
            link(dve.tensor_tensor(w3v[1], w3v[1], over_n(over2), ALU.mult))
            link(dve.tensor_tensor(w3v[2], w3v[0], w3v[1], ALU.add))
            link(dve.tensor_reduce(rt[0:1, 18, 16:32], w3v[2], AX.X, ALU.add))
            link(dve.tensor_scalar(rt[0:1, 19, 0:16], rt[0:1, 18, 16:32], 2.0 * EC, 2.0 * EC, ALU.mult, ALU.add))
            link(dve.tensor_scalar(rt[0:1, 19, 16:32], rt[0:1, 18, 16:32], 0.0, None, ALU.mult))
            link(dve.tensor_tensor_scan(rtw[0:1, 3, 0:16], rt[0:1, 19, 0:16], rt[0:1, 19, 16:32], 0.0,
                                        ALU.add, ALU.add))
            link(dve.tensor_copy(items[0:1, 33:48], rtw[0:1, 3, 0:15]))
            link(dve.tensor_copy(items[0:1, 32:33], incl[0:1, NE - 1:NE]))
            dve.tensor_copy(items[0:1, 0:32], rt[0:1, 18, :]).then_inc(items_ready, 1)
            dve.wait_ge(items_ready, 1)

            slot_hi = [w_his[:, (MOE0 + j) % 3, :] for j in range(3)] + [w_hi2[:, j, :] for j in range(3)]
            slot_lo = [w_los[:, (MOE0 + j) % 3, :] for j in range(3)] + [w_lo2[:, j, :] for j in range(3)]

            def rest_ahead(j, q1):
                n = MOE0 + j
                dve.wait_ge(w_hi_done, q1 * 6 + (n + 1))
                dve.tensor_tensor(slot_lo[j], raw[:, n % 3, :], f32(slot_hi[j]), ALU.subtract) \
                    .then_inc(w_lo_done, 1)

            def hidden(b, count, q, v, early=False):
                dve.wait_ge(se_ready[b], count + 1)
                if early:
                    dve.wait_ge(u_done, v + 1)
                else:
                    dve.wait_ge(w_used, q * 6 + (MOE0 + 4))
                dve.tensor_tensor(hid_e[:, b, :], silu_e[:, b, :], ps[:, 2 * b + 1, :], ALU.mult) \
                    .then_inc(he_ready[b], 1)

            def turned(b, count):
                dve.wait_ge(ht_hi_done[b], count + 1)
                dve.tensor_tensor(ht_lo[:, b, :, :].rearrange("p f t -> p (f t)"), ps[:, 4, :],
                                  f32(ht_hi[:, b, :, :].rearrange("p f t -> p (f t)")), ALU.subtract) \
                    .then_inc(ht_lo_done[b], 1)

            def add(b, half, q, v, last=False):
                bank = ((5, 6), (7, 5))[b][half]
                if last:
                    dve.wait_ge(w_used, q * 6 + (MOE0 + 6))
                else:
                    dve.wait_ge(ye_done, v * 2 + q + (2 * b + half + 1))
                s_ = slice(half * 512, (half + 1) * 512)
                dve.tensor_tensor(yacc[:, b, s_], yacc[:, b, s_], ps[:, bank, :], ALU.add).then_inc(ye_added, 1)

            for j in range(6):
                rest_ahead(j, 0)
            dve.sem_inc(ye_added, 1)
            n_items = dve.value_load(items[0:1, 32:33], min_val=1, max_val=MAX_ITEMS)
            pairs = dve.alloc_register("dve_pairs")
            dve.reg_mov(pairs, 0)
            with dve.Fori(0, n_items) as n:
                for b in range(2):
                    dve.wait_ge(xt_hi_done, n * 2 + (b + 1))
                    dve.tensor_tensor(xt_lo[:, b, :, :].rearrange("p k t -> p (k t)"),
                                      ps[:, 2 * b:2 * b + 2, :].rearrange("p a t -> p (a t)"),
                                      f32(xt_hi[:, b, :, :].rearrange("p k t -> p (k t)")), ALU.subtract) \
                        .then_inc(xt_lo_done, 1)
                dve.wait_ge(yacc_free, n + 1)
                dve.memset(yacc[:, :, :], 0.0).then_inc(yacc_zeroed, 1)
                dve.wait_ge(yacc_zeroed, n + 1)
                two = dve.value_load(items[0:1, bass.ds(n + 16, 1)], min_val=0, max_val=1)
                with dve.Fori(0, EC) as c:
                    q = n * EC + c
                    v = dve.snap(pairs, min_val=0, max_val=EC * MAX_ITEMS)
                    with dve.If(two > 0):
                        hidden(0, q, q, v, early=True)
                        rest_ahead(0, q + 1)
                        rest_ahead(1, q + 1)
                        turned(0, q)
                        rest_ahead(2, q + 1)
                        hidden(1, v, q, v)
                        rest_ahead(3, q + 1)
                        turned(1, v)
                        add(0, 0, q, v)
                        add(0, 1, q, v)
                        add(1, 0, q, v)
                        add(1, 1, q, v, last=True)
                        rest_ahead(4, q + 1)
                        rest_ahead(5, q + 1)
                        dve.reg_add(pairs, pairs, 1)
                    with dve.Else():
                        rest_ahead(0, q + 1)
                        rest_ahead(1, q + 1)
                        hidden(0, q, q, v)
                        turned(0, q)
                        rest_ahead(2, q + 1)
                        rest_ahead(3, q + 1)
                        add(0, 0, q, v)
                        add(0, 1, q, v, last=True)
                        rest_ahead(4, q + 1)
                        rest_ahead(5, q + 1)

            for i in range(NT):
                for j, g in enumerate((g1, g2)):
                    dve.wait_ge(comb_loaded[2 * i + j], 16)
                    ins = dve.scalar_tensor_tensor(h[:, i, :], comb[2 * i + j][:, :], g[:, i:i + 1], h[:, i, :],
                                                   ALU.mult, ALU.add)
                    if j:
                        ins.then_inc(h_ready, 1)
                    else:
                        link(ins)
            norm(4)


_INS = ["x", "w_in", "w_out", "ffn_w_gate", "ffn_w_up", "ffn_w_down", "moe_w_router", "moe_w1",
        "moe_w3", "moe_w2", "norm_rows", "params", "ident", "masks", "moe_const", "zeros"]


def lay_out(inputs):
    a = {k: np.ascontiguousarray(v) for k, v in inputs.items()}

    def cols(v):
        return v.reshape(-1, P).T

    packed = []
    for layer in range(DEPTH):
        par = np.zeros((P, NPAR), np.float32)

        def put(name, v):
            par[:, COLS[name]:COLS[name] + v.shape[1]] = v

        put("conv_w", cols(a["lru_conv_w"][layer]))
        put("conv_b", cols(a["lru_conv_b"][layer]))
        put("b_a", cols(a["lru_b_a"][layer]))
        put("b_x", cols(a["lru_b_x"][layer]))
        put("lam", cols(a["lru_lambda"][layer]))
        put("hlb", cols(a["hgrn_lower_bounds"]))
        put("pool_scale", cols(a["pool_scale"][layer]))
        put("sconv_w", cols(a["sconv_w"][layer]))
        put("norm_g", np.broadcast_to(np.tile(a["hgrn_norm_g"][layer], NH), (P, GW)))
        for name, w in (("bd_a", a["lru_w_a"]), ("bd_x", a["lru_w_x"]), ("bd_p", a["pool_w"])):
            for hd in range(NH):
                lo, ct = HD * (hd % 2), hd // 2
                c0 = COLS[name] + ct * P + lo
                par[lo:lo + HD, c0:c0 + HD] = w[layer, hd]
        for ct in range(CT):
            for half in range(2):
                win = 2 << (2 * ct + half)
                ramp = [win / min(t + 1, win) for t in range(16)]
                par[half * HD:(half + 1) * HD, COLS["ramp"] + ct * 16:COLS["ramp"] + (ct + 1) * 16] = ramp
        packed.append(par)

    masks = np.zeros((P, LEVELS, P), np.float32)
    s, t = np.arange(P)[:, None], np.arange(P)[None, :]
    masks[:, 0] = s == t
    for lv in range(1, LEVELS):
        half = 1 << (lv - 1)
        masks[:, lv] = (s // (2 * half) == t // (2 * half)) & (s // half % 2 == 0) & (t // half % 2 == 1)

    mc = np.zeros((P, NMC), np.float32)
    mc[:, MC_ONES:MC_ONES + P] = 1
    mc[:, MC_LOWER:MC_LOWER + P] = s < t
    mc[:, MC_IOTA:MC_IOTA + NE] = np.arange(NE) - NE
    mc[:, MC_TOK:MC_TOK + NT] = s + P * np.arange(NT)
    mc[:, MC_N:MC_N + 128] = np.arange(128) // NE
    mc[:, MC_E:MC_E + NE] = np.arange(NE)
    norm_rows = np.stack([a["norm_mix_g"][0], a["norm_ffn_g"][0], a["norm_mix_g"][1], a["norm_ffn_g"][1],
                          a["final_norm_g"]])
    a.update(norm_rows=norm_rows, params=np.stack(packed), ident=np.eye(P, dtype=np.float32), masks=masks,
             moe_const=mc, zeros=np.zeros(((2 * MAX_ITEMS + 2) * P, 1), np.uint32))
    return {k: a[k] for k in _INS}


def kernel(**inputs):
    import concourse.bacc as _bacc
    from concourse.bass_utils import run_bass_kernel_spmd as _run

    nc = _bacc.Bacc("TRN2", target_bir_lowering=False, num_devices=1)
    arrays, args = {}, []
    for name, a in lay_out(inputs).items():
        a = np.ascontiguousarray(a)
        arrays[f"in_{name}_dram"] = a
        args.append(nc.dram_tensor(f"in_{name}_dram", a.shape, mybir.dt.from_np(a.dtype), kind="ExternalInput").ap())
    args.append(nc.dram_tensor("out_0_dram", (1, T, D), F32, kind="ExternalOutput").ap())
    build(nc, *args)
    r = _run(nc, [arrays], core_ids=[0])
    return r.results[0]["out_0_dram"]
```

```python
from contextlib import ExitStack

import numpy as np

import concourse.bass as bass
from concourse import mybir

F32 = mybir.dt.float32
F32R = mybir.dt.float32r
I32 = mybir.dt.int32
U32 = mybir.dt.uint32
U8 = mybir.dt.uint8
ALU = mybir.AluOpType
ACT = mybir.ActivationFunctionType
AX = mybir.AxisListType

P = 128
D = 1024
KT = D // P
T = 512
NT = T // P
DEPTH = 2
GW = 256
CT = GW // P
NH = 4
HD = 64
FF = 2816
NE = 8
FE = 3584
EPS = 1e-6
HEAD_EPS = 1e-5
PIECE = 2048

A_X, A_G, Q, FG, V, O_G, PL, SB, SC, SX = range(10)
ORDER = [FG, Q, V, A_X, O_G, A_G, SC, SX, SB, PL]
N_IN = len(ORDER)
N_OUT = D // GW
DC = FF // GW
DENSE0 = N_IN + N_OUT
LAYER1 = DENSE0 + 3 * DC
MOE0 = LAYER1 + N_IN + N_OUT
CW = 512
EC = FE // CW
NARROW = P // 2
IP = 6 * EC
AHEAD = 4
ROWS = 2 * P
MAX_ITEMS = (2 * T + NE * (ROWS - 1)) // ROWS
MIN_ITEMS = 2 * T // ROWS
LEVELS = 8

LRU_SCONV, POOLED, HGRN = (6, 7, 0, 1), (4, 5), (2, 3)
RING = [(s, u) for s in ORDER[:6] for u in range(2)] + [("gate", u) for u in range(4)] \
    + [(s, u) for s in ORDER[6:] for u in range(2)]

COLS = {}
_at = 0
for _name, _n in (("conv_w", 8), ("conv_b", 2), ("b_a", 2), ("b_x", 2), ("lam", 2), ("hlb", 4),
                  ("pool_scale", 2), ("sconv_w", 6), ("ramp", 32), ("norm_g", 256),
                  ("bd_a", 256), ("bd_x", 256), ("bd_p", 256)):
    COLS[_name] = _at
    _at += _n
NPAR = _at
MC_ONES, MC_LOWER, MC_IOTA, MC_ZERO, MC_TOK, MC_N, MC_E = 0, 128, 256, 264, 272, 276, 404
NMC = 404 + 8


class At:
    def __init__(self, pieces, thirds):
        self.pieces, self.thirds = pieces, thirds


def build(nc, x, w_in, w_out, w_gate, w_up, w_down, w_router, w1, w3, w2, norm_rows, params, ident,
          masks, moe_const, zeros, out):
    ctx = ExitStack()
    with ctx:
        base = [(nc.sbuf_base + 63) // 64 * 64]

        def at(name, shape, dt, offset):
            return nc.alloc_sbuf_tensor_at(name, shape, dt, offset=offset)

        def size(shape, dt):
            n = 1
            for s in shape[1:]:
                n *= s
            return (n * (1 if dt == U8 else 4) + 31) // 32 * 32

        def sb(name, shape, dt=F32):
            t = at(name, shape, dt, base[0])
            base[0] += size(shape, dt)
            return t

        def sem(name):
            return ctx.enter_context(nc.semaphore(name))

        raw = sb("raw", [P, 3, PIECE])
        w_his = sb("w_hi", [P, 3, PIECE], F32R)
        w_los = sb("w_lo", [P, 3, PIECE], F32R)
        h = sb("h", [P, NT, D])
        acts0 = base[0]
        act_hi = sb("act_hi", [P, KT, T], F32R)
        act_lo = sb("act_lo", [P, KT, T], F32R)
        idt = sb("idt", [P, P])
        mask = sb("mask", [P, LEVELS, P], U8)
        par = sb("par", [P, NPAR])
        state = sb("state", [P, NT, CT, HD])
        small = sb("small", [P, 96])
        ssq, var, rstd = small[:, 0:4], small[:, 4:8], small[:, 8:12]
        coef = small[:, 12:14]
        lbs = small[:, 14:16]
        omlb = small[:, 16:18]
        eg_last = small[:, 18:26].rearrange("p (c n) -> p c n", c=CT)
        o_ssq, o_var, o_rstd = small[:, 26:42], small[:, 42:58], small[:, 58:74]
        tmp = small[:, 74:96]

        mix0 = base[0]
        full = [P, CT, T]
        keys = sb("keys", full)
        decay = sb("decay", full)
        qf = sb("qf", full)
        ex = [sb(f"ex{i}", full) for i in range(2)]
        xs = [sb(f"xs{i}", full) for i in range(2)]
        scores = sb("scores", [P, NH, NT, P])
        vals = sb("vals", [P, NT, GW])
        ogate = sb("ogate", [P, NT, GW])
        lru_in = sb("lru_in", [P, CT, T + 16])
        w1b = sb("win1", [P, CT, T + 16])
        w2b = sb("win2", [P, CT, T + 16])
        agate = sb("agate", full)
        igate = sb("igate", full)
        mult = sb("mult", full)
        scv = sb("scv", full)
        sxv = sb("sxv", [P, CT, T + 2])
        assert base[0] <= nc.sbuf_usable_end, (base[0], nc.sbuf_usable_end)
        grow = xs[0].rearrange("p c t -> p (c t)")
        rows = [e.rearrange("p c t -> p (c t)") for e in (ex[0], ex[1], decay, keys)]

        def rows_of(m, i):
            return rows[i if m == 3 else i % 2]

        x_in = w1b[:, :, 0:T]
        r_gate = w2b[:, :, 0:T]
        tanh_l = lru_in[:, :, 0:T]

        d0 = mix0
        silu_d = at("silu_d", [P, 2, T], F32, d0)
        hid_d = at("hid_d", [P, 2, T], F32, d0 + 4096)
        hid_hi = at("hid_hi", [P, 2, T], F32R, d0 + 8192)
        o = (mix0 + 7 * 4096)
        hid_lo = at("hid_lo", [P, 2, T], F32R, o)

        base[0] = acts0
        xt = sb("xt", [P, 2, KT, 2, P], F32R)
        silu_e = sb("silu_e", [P, 2, CW])
        hid_e = sb("hid_e", [P, 2, CW])
        ht = sb("ht", [P, 2, 4, 2, P], F32R)
        assert base[0] <= acts0 + 32768
        base[0] = mix0
        w_hi2 = sb("w_hi2", [P, 3, PIECE], F32R)
        w_lo2 = sb("w_lo2", [P, 3, PIECE], F32R)
        comb = [at(f"comb{i}", [P, D], F32, mix0 + i * 4096) for i in range(8)]
        yacc = sb("yacc", [P, 2, D])
        xg = [sb(f"xg{i}", [P, D]) for i in range(2)]
        growf = sb("growf", [P, D])
        mcon = sb("mcon", [P, NMC])
        wr = sb("wr", [P, KT, NE])
        idx = sb("idx", [P, 2 * MAX_ITEMS + 2], U32)
        col = sb("col", [P, 2], U32)
        slots = sb("slots", [P, NT, 2], U32)
        tokens = sb("tokens", [P, NT], U32)
        items = sb("items", [1, 64], I32)
        rt = sb("rt", [P, 20, NT * NE])
        rtw = sb("rtw", [1, 5, 128])
        fold0 = base[0]
        fold = sb("fold", [P, 2, CW])
        wr_hi = at("wr_hi", [P, KT, NE], F32R, fold0 + 2048)
        wr_lo = at("wr_lo", [P, KT, NE], F32R, fold0 + 2048 + 256)
        assert base[0] <= nc.sbuf_usable_end

        ps = ctx.enter_context(nc.psum_tensor("ps", [P, 8, 512], F32))

        hn_dram = nc.dram_tensor("hn_rows", (T, D), F32, kind="Internal").ap()
        y_dram = nc.dram_tensor("y_rows", (MAX_ITEMS * ROWS, D), F32, kind="Internal").ap()
        idx_dram = nc.dram_tensor("row_tokens", ((2 * MAX_ITEMS + 2) * P, 1), U32, kind="Internal").ap()

        raw_loaded = [sem(f"raw_loaded{i}") for i in range(3)]
        w_hi_done = sem("w_hi_done")
        w_lo_done = sem("w_lo_done")
        w_used = sem("w_used")
        const_loaded = sem("const_loaded")
        masks_loaded = sem("masks_loaded")
        mask_ready = sem("mask_ready")
        par_loaded = sem("par_loaded")
        grow_loaded = sem("grow_loaded")
        x_loaded = [sem(f"x_loaded{i}") for i in range(NT)]
        act_chain = sem("act_chain")
        dve_chain = sem("dve_chain")
        h_ready = sem("h_ready")
        ssq_done = sem("ssq_done")
        var_done = sem("var_done")
        sd_done = sem("sd_done")
        rows_done = sem("rows_done")
        tr_done = sem("tr_done")
        in_hi = sem("in_hi")
        in_lo = sem("in_lo")
        half_done = sem("half_done")
        gate_done = sem("gate_done")
        pool_done = sem("pool_done")
        ax_read = sem("ax_read")
        sx_read = sem("sx_read")
        sb_read = sem("sb_read")
        pl_read = sem("pl_read")
        par_act = sem("par_act")
        par_dve = sem("par_dve")
        e_ready = sem("e_ready")
        ln_ready = sem("ln_ready")
        qf_ready = sem("qf_ready")
        ex_ready = sem("ex_ready")
        exp_done = sem("exp_done")
        xs_ready = sem("xs_ready")
        level_done = sem("level_done")
        level_read = sem("level_read")
        v_ready = sem("v_ready")
        og_ready = sem("og_ready")
        ag_ready = sem("ag_ready")
        xin_ready = sem("xin_ready")
        gates_ready = sem("gates_ready")
        ta_ready = sem("ta_ready")
        m2_ready = sem("m2_ready")
        mult_ready = sem("mult_ready")
        sc_ready = sem("sc_ready")
        pd_ready = sem("pd_ready")
        gl_ready = sem("gl_ready")
        eg_done = sem("eg_done")
        kl_ready = sem("kl_ready")
        klt_done = sem("klt_done")
        klt_ready = sem("klt_ready")
        ds_done = sem("ds_done")
        st_ready = sem("st_ready")
        o_done = sem("o_done")
        osq_done = sem("osq_done")
        ovar_done = sem("ovar_done")
        osd_done = sem("osd_done")
        on_ready = sem("on_ready")
        ybt_done = sem("ybt_done")
        y_ready = sem("y_ready")
        y_hi = sem("y_hi")
        y_lo = sem("y_lo")
        out_done = sem("out_done")
        gu_done = sem("gu_done")
        s_ready = sem("s_ready")
        hid_ready = sem("hid_ready")
        hid_lo_ready = sem("hid_lo_ready")
        hid_hi_sem = sem("hid_hi_done")
        down_done = sem("down_done")
        down_added = sem("down_added")
        hn_stored = [sem(f"hn_stored{i}") for i in range(2)]
        moe_const_loaded = sem("moe_const_loaded")
        wr_split = sem("wr_split")
        logits_turned = sem("logits_turned")
        logits_copied = sem("logits_copied")
        logits_done = sem("logits_done")
        route_ready = sem("route_ready")
        rank_done = sem("rank_done")
        slots_ready = sem("slots_ready")
        items_ready = sem("items_ready")
        idx_zeroed = sem("idx_zeroed")
        scattered = sem("scattered")
        idx_loaded = sem("idx_loaded")
        col_ready = sem("col_ready")
        xg_loaded = [sem(f"xg_loaded{i}") for i in range(2)]
        xt_tr = sem("xt_tr")
        xt_hi_done = sem("xt_hi_done")
        xt_lo_done = sem("xt_lo_done")
        g_done = sem("g_done")
        u_done = sem("u_done")
        half_copied = sem("half_copied")
        gate_folded = sem("gate_folded")
        up_folded = sem("up_folded")
        y_moved = sem("y_moved")
        y_folded = sem("y_folded")
        gain_loaded = sem("gain_loaded")
        se_ready = [sem(f"se_ready{i}") for i in range(2)]
        he_ready = [sem(f"he_ready{i}") for i in range(2)]
        t_done = [sem(f"t_done{i}") for i in range(2)]
        ht_hi_done = [sem(f"ht_hi_done{i}") for i in range(2)]
        ht_lo_done = [sem(f"ht_lo_done{i}") for i in range(2)]
        ye_done = sem("ye_done")
        ye_added = sem("ye_added")
        y_stored = sem("y_stored")
        yacc_free = sem("yacc_free")
        mult_zeroed = sem("mult_zeroed")
        y_zeroed = sem("y_zeroed")
        comb_loaded = [sem(f"comb_loaded{i}") for i in range(8)]
        out_rows = sem("out_rows")
        out_stored = [sem(f"out_stored{i}") for i in range(2)]

        read_done = {FG: e_ready, Q: qf_ready, V: v_ready, A_X: ax_read, O_G: og_ready, A_G: ag_ready,
                     "gate": gates_ready, SC: sc_ready, SX: sx_read, SB: sb_read, PL: pl_read}

        def f32(ap):
            return ap.bitcast(F32)

        def pcol(name, i):
            return par[:, COLS[name] + i:COLS[name] + i + 1]

        def bank_of(key):
            return RING.index(key) % 4

        def output_done(eng, layer, key):
            s, u = key
            if s == "gate":
                eng.wait_ge(gate_done, 4 * layer + u + 1)
            elif u == 0:
                eng.wait_ge(half_done, N_IN * layer + ORDER.index(s) + 1)
            else:
                eng.wait_ge(w_used, layer * LAYER1 + ORDER.index(s) + 1)

        def bank_taken_over(eng, layer, key):
            n = RING.index(key) - 4
            if n >= 0:
                s, u = RING[n]
                eng.wait_ge(read_done[s], (4 if s == "gate" else 2) * layer + u + 1)

        def slice_of(dram, n, width=GW):
            return dram[:, n * width:(n + 1) * width].rearrange("(k p) n -> p k n", p=P)

        def raw3(slot, k=KT):
            return raw[:, slot, :].rearrange("p (k n) -> p k n", k=k)

        block = ctx.enter_context(nc.Block())

        @block.sync
        def _(sp):
            for i in range(NT):
                sp.dma_start(h[:, i, :], x[0, i * P:(i + 1) * P, :]).then_inc(x_loaded[i], 16)

            def load(n, src, k=KT):
                if n >= 3:
                    sp.wait_ge(w_lo_done, n - 2)
                sp.dma_start(raw3(n % 3, k), src).then_inc(raw_loaded[n % 3], 16)

            for layer in range(DEPTH):
                first = layer * LAYER1
                for i, s in enumerate(ORDER):
                    load(first + i, slice_of(w_in[layer], s))
                for j in range(N_OUT):
                    load(first + N_IN + j, slice_of(w_out[layer], j))
                if layer == 0:
                    with sp.Fori(0, DC) as c:
                        for j in range(3):
                            n = DENSE0 + j
                            sp.wait_ge(w_lo_done, c * 3 + (n - 2))
                            if j < 2:
                                src = (w_gate, w_up)[j][0][:, bass.ds(c * GW, GW)] \
                                    .rearrange("(k p) n -> p k n", p=P)
                                dst = raw3(n % 3)
                            else:
                                src = w_down[0][bass.ds(c * GW, GW), :] \
                                    .rearrange("(k p) n -> p k n", p=P)
                                dst = raw3(n % 3, 2)
                            sp.dma_start(dst, src).then_inc(raw_loaded[n % 3], 16)

            sp.wait_ge(items_ready, 1)
            n_items = sp.value_load(items[0:1, 32:33], min_val=1, max_val=MAX_ITEMS)
            with sp.Fori(0, n_items) as n:
                e = sp.value_load(items[0:1, bass.ds(n, 1)], min_val=0, max_val=NE - 1)

                def load_piece(p, c_, which):
                    kind, half = which
                    at_ = n * IP + p
                    sp.wait_ge(w_lo_done, at_ + (MOE0 - 2))
                    slot = (MOE0 + p_static[0]) % 3
                    if kind < 2:
                        src = (w1, w3)[kind][0][bass.ds(e, 1), half * 512:(half + 1) * 512,
                                                bass.ds(c_ * CW, CW)].rearrange("x (k p) n -> p (x k) n", p=P)
                        dst = raw3(slot, 4)
                    else:
                        src = w2[0][bass.ds(e, 1), bass.ds(c_ * CW + half * GW, GW), :] \
                            .rearrange("x (k p) n -> p (x k) n", p=P)
                        dst = raw3(slot, 2)
                    sp.dma_start(dst, src).then_inc(raw_loaded[slot], 16)
                    p_static[0] += 1

                p_static = [0]
                for p in range(2):
                    load_piece(p, 0, (p, 0))
                with sp.Fori(0, EC - 1) as c:
                    for j, (dc, which) in enumerate(((0, (0, 1)), (0, (1, 1)), (1, (0, 0)), (1, (1, 0)),
                                                     (0, (2, 0)), (0, (2, 1)))):
                        load_piece(c * 6 + (2 + j), c + dc, which)
                for j, which in enumerate(((0, 1), (1, 1), (2, 0), (2, 1))):
                    load_piece(IP - 4 + j, EC - 1, which)
            for j in range(AHEAD):
                sp.wait_ge(w_lo_done, n_items * IP + (MOE0 + j - 2))
                sp.sem_inc(raw_loaded[(MOE0 + j) % 3], 16)

            for i in range(NT):
                sp.wait_ge(out_rows, i + 1)
                sp.dma_start(out[0, i * P:(i + 1) * P, :], yacc[:, i % 2, :]).then_inc(out_stored[i % 2], 16)
            for i in range(2):
                sp.wait_ge(out_stored[i], 32)

        @block.gpsimd
        def _(pool):
            pool.dma_start(grow, norm_rows[0].partition_broadcast(P)).then_inc(grow_loaded, 16)
            pool.dma_start(idt[:, :], ident).then_inc(const_loaded, 16)
            pool.dma_start(par[:, :], params[0]).then_inc(par_loaded, 16)
            pool.dma_start(igate.rearrange("p c (l t) -> p (c l) t", t=P), masks).then_inc(masks_loaded, 16)
            pool.wait_ge(masks_loaded, 16)
            pool.tensor_copy(mask[:, :, :], igate.rearrange("p c (l t) -> p (c l) t", t=P)) \
                .then_inc(mask_ready, 1)
            pool.dma_start(idx_dram, zeros).then_inc(idx_zeroed, 16)
            pool.wait_ge(ds_done, 1)
            pool.dma_start(grow, norm_rows[1].partition_broadcast(P)).then_inc(grow_loaded, 16)
            pool.wait_ge(w_used, DENSE0)
            pool.dma_start(par[:, :], params[1]).then_inc(par_loaded, 16)
            pool.memset(mult[:, :, :], 0.0).then_inc(mult_zeroed, 1)
            pool.wait_ge(mult_zeroed, 1)
            rest = MAX_ITEMS - MIN_ITEMS
            pool.dma_start(y_dram[MIN_ITEMS * ROWS:, :].rearrange("(m p) d -> p m d", p=P),
                           mult.rearrange("p c t -> p (c t)").unsqueeze(1).broadcast_to([P, 2 * rest, D])) \
                .then_inc(y_zeroed, 16)
            pool.wait_ge(rows_done, 8)
            pool.dma_start(grow, norm_rows[2].partition_broadcast(P)).then_inc(grow_loaded, 16)
            pool.wait_ge(ds_done, 2)
            pool.dma_start(grow, norm_rows[3].partition_broadcast(P)).then_inc(grow_loaded, 16)
            pool.wait_ge(w_used, MOE0)
            pool.dma_start(mcon[:, :], moe_const).then_inc(moe_const_loaded, 16)
            pool.dma_start(wr[:, :, :], w_router[0].rearrange("(k p) e -> p k e", p=P)) \
                .then_inc(moe_const_loaded, 16)
            for i in range(NT):
                pool.wait_ge(rows_done, 12 + i + 1)
                pool.dma_start(hn_dram[i * P:(i + 1) * P, :], rows_of(3, i)).then_inc(hn_stored[i % 2], 16)

            pool.wait_ge(slots_ready, 1)
            pool.wait_ge(idx_zeroed, 16)
            for i in range(NT):
                for j in range(2):
                    pool.indirect_dma_start(
                        idx_dram, bass.IndirectOffsetOnAxis(ap=slots[:, i, j:j + 1], axis=0),
                        tokens[:, i:i + 1], None).then_inc(scattered, 16)
            pool.wait_ge(scattered, 16 * 2 * NT)
            by_block = idx_dram.rearrange("(m p) o -> p (m o)", p=P)
            pool.dma_start(idx[:, 0:2], by_block[:, 0:2],
                           allow_slow_non_contiguous=True).then_inc(idx_loaded, 16)
            pool.wait_ge(idx_loaded, 16)
            for i in range(2):
                pool.wait_ge(hn_stored[i], 32)

            def gather(n, b):
                pool.tensor_copy(col[:, b:b + 1], idx[:, bass.ds(n * 2 + b, 1)]).then_inc(col_ready, 1)
                pool.wait_ge(col_ready, n * 2 + (b + 1))
                pool.nop(nofuse=True)
                pool.indirect_dma_start(xg[b][:, :], None, hn_dram,
                                        bass.IndirectOffsetOnAxis(ap=col[:, b:b + 1], axis=0)) \
                    .then_inc(xg_loaded[b], 16)

            for b in range(2):
                pool.tensor_copy(col[:, b:b + 1], idx[:, b:b + 1]).then_inc(col_ready, 1)
                pool.wait_ge(col_ready, b + 1)
                pool.indirect_dma_start(xg[b][:, :], None, hn_dram,
                                        bass.IndirectOffsetOnAxis(ap=col[:, b:b + 1], axis=0)) \
                    .then_inc(xg_loaded[b], 16)
            pool.dma_start(idx[:, 2:], by_block[:, 2:],
                           allow_slow_non_contiguous=True).then_inc(idx_loaded, 16)
            pool.wait_ge(idx_loaded, 32)
            pool.wait_ge(y_zeroed, 16)
            pool.memset(yacc[:, :, :], 0.0).then_inc(yacc_free, 1)
            pool.wait_ge(items_ready, 1)
            n_items = pool.value_load(items[0:1, 32:33], min_val=1, max_val=MAX_ITEMS)
            narrows = pool.alloc_register("pool_narrows")
            pool.reg_mov(narrows, 0)
            with pool.Fori(0, n_items) as n:
                for b in range(2):
                    pool.wait_ge(xt_tr, n * 2 + (b + 1))
                    gather(n + 1, b)
                pool.wait_ge(ye_added, pool.value_load(items[0:1, bass.ds(n + 33, 1)], min_val=1,
                                                       max_val=4 * EC * MAX_ITEMS) + 1)
                pool.nop(nofuse=True)
                narrow = pool.value_load(items[0:1, bass.ds(n + 48, 1)], min_val=0, max_val=1)
                with pool.If(narrow > 0):
                    pool.dma_start(growf[0:NARROW, :], yacc[NARROW:P, 1, :]).then_inc(y_moved, 16)
                    pool.wait_ge(y_moved, pool.snap(narrows, min_val=0, max_val=MAX_ITEMS) * 16 + 16)
                    pool.reg_add(narrows, narrows, 1)
                    pool.nop(nofuse=True)
                    pool.tensor_tensor(yacc[0:NARROW, 1, :], yacc[0:NARROW, 1, :], growf[0:NARROW, :], ALU.add) \
                        .then_inc(y_folded, 1)
                with pool.Else():
                    pool.sem_inc(y_folded, 1)
                pool.wait_ge(y_folded, n + 1)
                pool.nop(nofuse=True)
                pool.dma_start(y_dram[bass.ds(n * ROWS, ROWS), :].rearrange("(b p) d -> p b d", p=P),
                               yacc[:, :, :]).then_inc(y_stored, 16)
                pool.wait_ge(y_stored, n * 16 + 16)
                pool.nop(nofuse=True)
                pool.memset(yacc[:, :, :], 0.0).then_inc(yacc_free, 1)
            pool.dma_start(growf[:, :], norm_rows[4].partition_broadcast(P)).then_inc(gain_loaded, 16)
            pool.wait_ge(w_lo_done, n_items * IP + (MOE0 + AHEAD))
            for b in range(2):
                pool.wait_ge(xg_loaded[b], n_items * 16 + 16)
            pool.nop(nofuse=True)
            for i in range(NT):
                for j in range(2):
                    pool.indirect_dma_start(comb[2 * i + j][:, :], None, y_dram,
                                            bass.IndirectOffsetOnAxis(ap=slots[:, i, j:j + 1], axis=0)) \
                        .then_inc(comb_loaded[2 * i + j], 16)

        @block.tensor
        def _(pe):
            def mm3(o_, lhi, llo, rhi, rlo, start, stop):
                pe.matmul(o_, lhi, rhi, start=start, stop=False)
                pe.matmul(o_, lhi, rlo, start=False, stop=False)
                return pe.matmul(o_, llo, rhi, start=False, stop=stop)

            def both_parts(t, b, k):
                return t[:, b, k].rearrange("p a t -> p (a t)")[:, NARROW:NARROW + P]

            def mm2(o_, both, whi_, wlo_, start, stop):
                pe.matmul(o_, both, whi_, start=start, stop=False)
                return pe.matmul(o_, both, wlo_, start=False, stop=stop)

            def whi(n, k=KT):
                return w_his[:, n % 3, :].rearrange("p (k n) -> p k n", k=k)

            def wlo(n, k=KT):
                return w_los[:, n % 3, :].rearrange("p (k n) -> p k n", k=k)

            def norm_transposes(m):
                for i in range(NT):
                    pe.wait_ge(rows_done, 4 * m + i + 1)
                    for k in range(KT):
                        if i == 0 and k >= 4 and m % 2:
                            pe.wait_ge(h_ready, 4 * (m // 2) + k - 3)
                        if i == 0 and k in (4, 6) and m == 2:
                            pe.wait_ge(down_added, 4 * DC + k // 2 + 1)
                        last = pe.transpose(ps[:, k, i * P:(i + 1) * P], rows_of(m, i)[:, k * P:(k + 1) * P],
                                            idt[:, :])
                    last.then_inc(tr_done, 1)

            def project(layer, i):
                s, n = ORDER[i], layer * LAYER1 + i
                pe.wait_ge(w_lo_done, n + 1)
                for u in range(2):
                    bank = bank_of((s, u))
                    bank_taken_over(pe, layer, (s, u))
                    if s in (V, O_G):
                        for t in range(2):
                            tt = 2 * u + t
                            for k in range(KT):
                                last = mm3(ps[:, bank, t * GW:(t + 1) * GW],
                                           act_hi[:, k, tt * P:(tt + 1) * P], act_lo[:, k, tt * P:(tt + 1) * P],
                                           whi(n)[:, k, :], wlo(n)[:, k, :], k == 0, k == KT - 1)
                    else:
                        for k in range(KT):
                            if i == 0 and u == 0:
                                pe.wait_ge(in_lo, (2 * layer) * KT + k + 1)
                            last = mm3(ps[:, bank, :], whi(n)[:, k, u * P:(u + 1) * P],
                                       wlo(n)[:, k, u * P:(u + 1) * P], act_hi[:, k, :], act_lo[:, k, :],
                                       k == 0, k == KT - 1)
                    last.then_inc((half_done, w_used)[u], 1)

            def level(layer, lv):
                pe.wait_ge(xs_ready, layer * LEVELS + lv + 1)
                if lv == 0:
                    pe.wait_ge(qf_ready, 2 * layer + 2)
                for hd in range(NH):
                    lo = HD * (hd % 2)
                    if lv:
                        pe.wait_ge(level_read, 4 * (layer * LEVELS + lv - 1) + hd + 1)
                    for c in range(NT):
                        if lv:
                            a = b = xs[lv % 2][lo:lo + HD, hd // 2, c * P:(c + 1) * P]
                        else:
                            a = keys[lo:lo + HD, hd // 2, c * P:(c + 1) * P]
                            b = qf[lo:lo + HD, hd // 2, c * P:(c + 1) * P]
                        last = pe.matmul(ps[:, 4 + hd, c * P:(c + 1) * P], a, b, start=True, stop=True)
                    last.then_inc(level_done, 1)

            def gates(layer):
                pe.wait_ge(xin_ready, layer + 1)
                for u in range(4):
                    bank = bank_of(("gate", u))
                    bank_taken_over(pe, layer, ("gate", u))
                    c0 = COLS[("bd_a", "bd_x")[u // 2]] + (u % 2) * P
                    pe.matmul(ps[:, bank, :], par[:, c0:c0 + P], x_in[:, u % 2, :], start=True, stop=True) \
                        .then_inc(gate_done, 1)

            def pool_product(layer, u):
                pe.wait_ge(pd_ready, layer + 1)
                c0 = COLS["bd_p"] + u * P
                pe.matmul(ps[:, 5 + u, :], par[:, c0:c0 + P], igate[:, u, :], start=True, stop=True) \
                    .then_inc(pool_done, 1)

            def output(layer, j, tiles, ks, stop=False):
                n = layer * LAYER1 + N_IN + j
                for tt in tiles:
                    for k in ks:
                        last = mm3(ps[:, tt + 4 * (j // 2), (j % 2) * GW:(j % 2 + 1) * GW],
                                   act_hi[:, k, tt * P:(tt + 1) * P], act_lo[:, k, tt * P:(tt + 1) * P],
                                   whi(n)[:, k, :], wlo(n)[:, k, :], j % 2 == 0 and k == LRU_SCONV[0],
                                   j % 2 == 1 and stop and k == ks[-1])
                    if stop:
                        last.then_inc(w_used if tt == NT - 1 else out_done, 1)

            def hgrn_tail(layer):
                first = layer * LAYER1 + N_IN
                pe.wait_ge(pl_read, 2 * (layer + 1))
                pe.wait_ge(y_lo, 4 * layer + 2)
                pe.wait_ge(w_lo_done, first + 1)
                output(layer, 0, range(NT), LRU_SCONV)
                pe.wait_ge(kl_ready, layer + 1)
                pe.wait_ge(level_read, 4 * LEVELS * (layer + 1))
                for c in range(NT - 1):
                    for ct in range(CT):
                        last = pe.transpose(ps[:, 4 + c // 2, (c % 2) * GW + ct * P:(c % 2) * GW + (ct + 1) * P],
                                            ex[1][:, ct, c * P:(c + 1) * P], idt[:, :])
                last.then_inc(klt_done, 1)
                pe.wait_ge(w_lo_done, first + 2)
                output(layer, 1, range(NT), LRU_SCONV)
                pe.wait_ge(klt_ready, layer + 1)
                pe.wait_ge(v_ready, 2 * layer + 2)
                klt = xs[0].rearrange("p c t -> p (c t)").rearrange("p (n g) -> p n g", g=GW)
                for c in range(NT - 1):
                    for hd in range(NH):
                        lo = HD * (hd % 2)
                        last = pe.matmul(ps[lo:lo + HD, 6, c * P + (hd // 2) * HD:c * P + (hd // 2 + 1) * HD],
                                         klt[:, c, hd * HD:(hd + 1) * HD], vals[:, c, hd * HD:(hd + 1) * HD],
                                         start=True, stop=True)
                last.then_inc(ds_done, 1)
                pool_product(layer, 0)
                for c in range(NT):
                    if c:
                        pe.wait_ge(st_ready, (NT - 1) * layer + c)
                    if c == NT - 1:
                        pool_product(layer, 1)
                    for hd in range(NH):
                        lo, ct = HD * (hd % 2), hd // 2
                        o_ = ps[:, (7, 4)[hd % 2], c * P + ct * HD:c * P + (ct + 1) * HD]
                        last = pe.matmul(o_, scores[:, hd, c, :], vals[:, c, hd * HD:(hd + 1) * HD],
                                         start=True, stop=c == 0)
                        if c:
                            last = pe.matmul(o_, ex[0][lo:lo + HD, ct, c * P:(c + 1) * P],
                                             state[lo:lo + HD, c, ct, :], start=False, stop=True)
                last.then_inc(o_done, 1)
                pe.wait_ge(y_lo, 4 * layer + 3)
                for j in range(2):
                    output(layer, j, range(NT), POOLED)
                pe.wait_ge(w_lo_done, first + 3)
                output(layer, 2, (1,), LRU_SCONV + POOLED)
                pe.wait_ge(on_ready, layer + 1)
                on = xs[1].rearrange("p c t -> p (c t)").rearrange("p (n g) -> p n g", g=GW)
                for ct in range(CT):
                    for c in range(NT):
                        last = pe.transpose(ps[:, (4, 7)[ct], c * P:(c + 1) * P], on[:, c, ct * P:(ct + 1) * P],
                                            idt[:, :])
                last.then_inc(ybt_done, 1)
                output(layer, 2, (2,), LRU_SCONV + POOLED)
                pe.wait_ge(y_lo, 4 * (layer + 1))
                for j in range(2):
                    output(layer, j, range(NT), HGRN, stop=True)
                output(layer, 2, (0,), LRU_SCONV + POOLED + HGRN, stop=True)
                output(layer, 2, (1, 2), HGRN, stop=True)
                output(layer, 2, (3,), LRU_SCONV + POOLED + HGRN, stop=True)
                pe.wait_ge(w_lo_done, first + 4)
                output(layer, 3, range(NT), LRU_SCONV + POOLED + HGRN, stop=True)

            def dense_chunk(c):
                for j in range(2):
                    n = DENSE0 + j
                    pe.wait_ge(w_lo_done, c * 3 + (n + 1))
                    for ft in range(2):
                        for k in range(KT):
                            if j == 0 and ft == 0:
                                pe.wait_ge(in_lo, KT + k + 1)
                            last = mm3(ps[:, 2 * j + ft, :], whi(n)[:, k, ft * P:(ft + 1) * P],
                                       wlo(n)[:, k, ft * P:(ft + 1) * P], act_hi[:, k, :], act_lo[:, k, :],
                                       k == 0, k == KT - 1)
                        last.then_inc((gu_done, w_used)[ft], 1)
                n = DENSE0 + 2
                pe.wait_ge(w_lo_done, c * 3 + (n + 1))
                for pair in range(2):
                    for ft in range(2):
                        if pair == 0:
                            pe.wait_ge(hid_lo_ready, c * 2 + (ft + 1))
                        for t in range(2):
                            tt = 2 * pair + t
                            if ft == 0:
                                pe.wait_ge(down_added, c * 4 + (tt + 3))
                            for half in range(2):
                                last = mm3(ps[:, 4 + 2 * t + half, :], hid_hi[:, ft, tt * P:(tt + 1) * P],
                                           hid_lo[:, ft, tt * P:(tt + 1) * P],
                                           whi(n, 2)[:, ft, half * 512:(half + 1) * 512],
                                           wlo(n, 2)[:, ft, half * 512:(half + 1) * 512], ft == 0, ft == 1)
                            if ft == 1:
                                last.then_inc(w_used if tt == NT - 1 else down_done, 1)

            pe.wait_ge(const_loaded, 16)
            for layer in range(DEPTH):
                norm_transposes(2 * layer)
                for i in range(N_IN):
                    project(layer, i)
                    if i >= 2:
                        level(layer, i - 2)
                    if i == 5:
                        gates(layer)
                hgrn_tail(layer)
                norm_transposes(2 * layer + 1)
                if layer == 0:
                    with pe.Fori(0, DC) as c:
                        dense_chunk(c)

            pe.wait_ge(wr_split, 2)
            for k in range(KT):
                pe.wait_ge(in_lo, 3 * KT + k + 1)
                last = mm3(ps[0:NE, 0, :], wr_hi[:, k, :], wr_lo[:, k, :], act_hi[:, k, :], act_lo[:, k, :],
                           k == 0, k == KT - 1)
            last.then_inc(logits_turned, 1)
            pe.wait_ge(logits_copied, 1)
            for tt in range(NT):
                last = pe.matmul(ps[:, 1, tt * NE:(tt + 1) * NE], fold[0:NE, 0, tt * P:(tt + 1) * P],
                                 idt[0:NE, 0:NE], start=True, stop=True)
            last.then_inc(logits_done, 1)
            pe.wait_ge(route_ready, 1)
            chosen = rt[:, 8, :].rearrange("p (t e) -> p t e", e=NE)
            for tt in range(NT):
                for j in range(tt + 1):
                    c0 = MC_LOWER if j == tt else MC_ONES
                    pe.matmul(ps[:, 3, tt * NE:(tt + 1) * NE], mcon[:, c0:c0 + P], chosen[:, j, :],
                              start=j == 0, stop=j == tt)
            for j in range(NT):
                last = pe.matmul(ps[:, 2, 0:NE], mcon[:, MC_ONES:MC_ONES + P], chosen[:, j, :],
                                 start=j == 0, stop=j == NT - 1)
            last.then_inc(rank_done, 1)

            slot_hi = [w_his[:, (MOE0 + j) % 3, :] for j in range(3)] + [w_hi2[:, j, :] for j in range(3)]
            slot_lo = [w_los[:, (MOE0 + j) % 3, :] for j in range(3)] + [w_lo2[:, j, :] for j in range(3)]

            def up(b, kind, half, p, c_at, release, narrow=False):
                pe.wait_ge(w_lo_done, c_at + (MOE0 + p + 1))
                hi_ = slot_hi[p % 6].rearrange("p (k n) -> p k n", k=4)
                lo_ = slot_lo[p % 6].rearrange("p (k n) -> p k n", k=4)
                for k in range(4):
                    start, stop = half == 0 and k == 0, half == 1 and k == 3
                    if narrow and b:
                        last = mm2(ps[:, 2 * b + kind, :], both_parts(xt, b, 4 * half + k),
                                   hi_[:, k, :], lo_[:, k, :], start, stop)
                    else:
                        last = mm3(ps[:, 2 * b + kind, :], xt[:, b, 4 * half + k, 0, :],
                                   xt[:, b, 4 * half + k, 1, :], hi_[:, k, :], lo_[:, k, :], start, stop)
                if release:
                    last.then_inc(w_used, 1)
                elif half == 1:
                    last.then_inc((g_done, u_done)[kind], 1)

            def turn(b, count, narrow=False):
                pe.wait_ge(he_ready[b], count + 1)
                m = NARROW if narrow and b else P
                if m < P:
                    pe.nop(nofuse=True)
                for f in range(4):
                    for o_ in range(f * P, (f + 1) * P, m):
                        last = pe.transpose(ps[:, 4, o_:o_ + m], hid_e[0:m, b, f * P:(f + 1) * P],
                                            idt[0:m, 0:m])
                last.then_inc(t_done[b], 1)

            def down(b, half, count, p, c_at, release, narrow=False):
                bank = ((5, 6), (7, 5))[b][half]
                if half == 0:
                    pe.wait_ge(ht_lo_done[b], count + 1)
                for f in range(4):
                    if f % 2 == 0 and half == 0:
                        pe.wait_ge(w_lo_done, c_at + (MOE0 + p + f // 2 + 1))
                    hi_ = slot_hi[(p + f // 2) % 6].rearrange("p (k n) -> p k n", k=2)
                    lo_ = slot_lo[(p + f // 2) % 6].rearrange("p (k n) -> p k n", k=2)
                    w_hi_, w_lo_ = (w[:, f % 2, half * 512:(half + 1) * 512] for w in (hi_, lo_))
                    if narrow and b:
                        last = mm2(ps[:, bank, :], both_parts(ht, b, f), w_hi_, w_lo_, f == 0, f == 3)
                    else:
                        last = mm3(ps[:, bank, :], ht[:, b, f, 0, :], ht[:, b, f, 1, :], w_hi_, w_lo_,
                                   f == 0, f == 3)
                if release and half == 1:
                    last.then_inc(w_used, 2)
                else:
                    last.then_inc(ye_done, 1)

            def turn_rows(b, n, m=P):
                pe.wait_ge(xg_loaded[b], n * 16 + 16)
                if m < P:
                    pe.nop(nofuse=True)
                for k in range(KT):
                    for o_ in range((k % 4) * P, (k % 4 + 1) * P, m):
                        last = pe.transpose(ps[:, 2 * b + k // 4, o_:o_ + m],
                                            xg[b][0:m, k * P:(k + 1) * P], idt[0:m, 0:m])
                last.then_inc(xt_tr, 1)

            def turn_next(n):
                turn_rows(0, n)
                narrow = pe.value_load(items[0:1, bass.ds(n + 48, 1)], min_val=0, max_val=1)
                with pe.If(narrow > 0):
                    turn_rows(1, n, NARROW)
                with pe.Else():
                    turn_rows(1, n)

            def chunk_two(n, c, q, v, last, narrow):
                at_ = n * IP + c * 6
                for b in range(2):
                    up(b, 0, 1, 2, at_, b == 1, narrow)
                    up(b, 1, 1, 3, at_, b == 1, narrow)
                if not last:
                    pe.wait_ge(se_ready[0], q + 1)
                    up(0, 0, 0, 4, at_, False, narrow)
                    pe.wait_ge(he_ready[0], q + 1)
                    up(0, 1, 0, 5, at_, False, narrow)
                    turn(0, q)
                    pe.wait_ge(se_ready[1], v + 1)
                    up(1, 0, 0, 4, at_, True, narrow)
                    pe.wait_ge(ht_lo_done[0], q + 1)
                    turn(1, v, narrow)
                    up(1, 1, 0, 5, at_, True, narrow)
                else:
                    turn(0, q)
                p = 4 if last else 6
                pe.wait_ge(ye_added, (q + v) * 2 + 1)
                down(0, 0, q, p, at_, False, narrow)
                if last:
                    turn(1, v, narrow)
                    turn_next(n + 1)
                down(0, 1, q, p, at_, False, narrow)
                down(1, 0, v, p, at_, False, narrow)
                pe.wait_ge(ye_added, (q + v) * 2 + 2)
                down(1, 1, v, p, at_, True, narrow)
                pe.reg_add(pairs, pairs, 1)

            def chunk_one(n, c, q, v, last):
                at_ = n * IP + c * 6
                for kind in range(2):
                    up(0, kind, 1, 2 + kind, at_, True)
                if not last:
                    pe.wait_ge(se_ready[0], q + 1)
                    up(0, 0, 0, 4, at_, True)
                    turn(0, q)
                    up(0, 1, 0, 5, at_, True)
                else:
                    turn(0, q)
                    turn_next(n + 1)
                p = 4 if last else 6
                pe.wait_ge(ye_added, (q + v) * 2 + 1)
                down(0, 0, q, p, at_, False)
                down(0, 1, q, p, at_, True)

            pe.wait_ge(items_ready, 1)
            turn_next(0)
            n_items = pe.value_load(items[0:1, 32:33], min_val=1, max_val=MAX_ITEMS)
            pairs = pe.alloc_register("pe_pairs")
            pe.reg_mov(pairs, 0)
            with pe.Fori(0, n_items) as n:
                pe.wait_ge(xt_lo_done, n * 2 + 2)
                two = pe.value_load(items[0:1, bass.ds(n + 16, 1)], min_val=0, max_val=1)
                narrow = pe.value_load(items[0:1, bass.ds(n + 48, 1)], min_val=0, max_val=1)

                def item_two(narrow):
                    for b in range(2):
                        for kind in range(2):
                            up(b, kind, 0, kind, n * IP, b == 1, narrow)
                    with pe.Fori(0, EC - 1) as c:
                        chunk_two(n, c, n * EC + c, pe.snap(pairs, min_val=0, max_val=EC * MAX_ITEMS),
                                  False, narrow)
                    chunk_two(n, EC - 1, n * EC + (EC - 1),
                              pe.snap(pairs, min_val=0, max_val=EC * MAX_ITEMS), True, narrow)

                with pe.If(two > 0):
                    with pe.If(narrow > 0):
                        item_two(True)
                    with pe.Else():
                        item_two(False)
                with pe.Else():
                    v = pe.snap(pairs, min_val=0, max_val=EC * MAX_ITEMS)
                    for kind in range(2):
                        up(0, kind, 0, kind, n * IP, True)
                    with pe.Fori(0, EC - 1) as c:
                        chunk_one(n, c, n * EC + c, v, False)
                    chunk_one(n, EC - 1, n * EC + (EC - 1), v, True)

        @block.scalar
        def _(act):
            chain = [0]

            def link(ins):
                chain[0] += 1
                ins.then_inc(act_chain, 1)
                act.wait_ge(act_chain, chain[0])

            def round_piece(n):
                act.wait_ge(raw_loaded[n % 3], 16 * (n // 3 + 1))
                if n >= 3:
                    act.wait_ge(w_used, n - 2)
                act.activation(w_his[:, n % 3, :], raw[:, n % 3, :], ACT.Copy).then_inc(w_hi_done, 1)

            def norm(m):
                junk = (xs[1] if m < 4 else silu_e).rearrange("p c t -> p (c t)")
                for i in range(NT):
                    if m == 0:
                        act.wait_ge(x_loaded[i], 16)
                    elif m == 2:
                        act.wait_ge(down_added, 4 * DC + i + 1)
                    else:
                        act.wait_ge(h_ready, 4 * (m // 2) + i + 1)
                    if i:
                        act.wait_ge(ssq_done, 4 * m + i)
                    act.activation(junk, h[:, i, :], ACT.Square, accum_out=ssq[:, i:i + 1]).then_inc(ssq_done, 1)
                    act.wait_ge(var_done, 4 * m + i + 1)
                    act.activation(var[:, i:i + 1], var[:, i:i + 1], ACT.Sqrt).then_inc(sd_done, 1)

            def norm_evac(m):
                act.wait_ge(tr_done, 4 * (m + 1))
                for k in range(KT):
                    act.activation(act_hi[:, k, :], ps[:, k, :], ACT.Copy).then_inc(in_hi, 1)

            def from_ring(layer, key, dst, func, **kw):
                output_done(act, layer, key)
                return act.activation(dst, ps[:, bank_of(key), :], func, **kw)

            def level_exp(layer, lv):
                act.wait_ge(ex_ready, 7 * layer + lv)
                e = ex[lv % 2]
                act.activation(e[:, :, :], e[:, :, :], ACT.Exp).then_inc(exp_done, 1)

            def mixers(layer):
                first = layer * LAYER1
                norm(2 * layer)
                if layer == 0:
                    round_piece(0)
                norm_evac(2 * layer)
                for n in (first + 2,) if layer else (1, 2):
                    round_piece(n)
                act.wait_ge(par_dve, 2 * layer + 1)
                act.activation(tmp[:, 0:6], tmp[:, 0:6], ACT.Exp).then_inc(par_act, 1)
                act.wait_ge(par_dve, 2 * layer + 2)
                act.wait_ge(e_ready, 2 * layer + 2)
                act.activation(keys[:, :, :], xs[1][:, :, :], ACT.Sigmoid).then_inc(ln_ready, 1)
                link(act.activation(xs[1][:, :, :], xs[1][:, :, :], ACT.Exp))
                for ct in range(CT):
                    act.activation(ex[0][:, ct, :], xs[1][:, ct, :], ACT.Ln, bias=1.0, scale=lbs[:, ct:ct + 1])
                act.activation(ex[1][:, :, :], xs[1][:, :, :], ACT.Ln, bias=1.0).then_inc(ln_ready, 1)
                for i in range(1, N_IN):
                    round_piece(first + i + 2)
                    if i < LEVELS:
                        level_exp(layer, i)
                    if i == 6:
                        for u in range(4):
                            dst = (r_gate, igate)[u // 2][:, u % 2, :]
                            ins = from_ring(layer, ("gate", u), dst, ACT.Sigmoid,
                                            bias=pcol(("b_a", "b_x")[u // 2], u % 2))
                            ins.then_inc(gates_ready, 1)
                        act.wait_ge(gates_ready, 4 * (layer + 1))
                        for ct in range(CT):
                            act.activation(tanh_l[:, ct, :], r_gate[:, ct, :], ACT.Tanh, scale=coef[:, ct:ct + 1]) \
                                .then_inc(ta_ready, 1)
                        for ct in range(CT):
                            act.activation(r_gate[:, ct, :], r_gate[:, ct, :], ACT.Exp, scale=coef[:, ct:ct + 1]) \
                                .then_inc(ta_ready, 1)
                    if i == 8:
                        act.wait_ge(m2_ready, layer + 1)
                        act.activation(mult[:, :, :], mult[:, :, :], ACT.Sqrt, scale=-1.0).then_inc(mult_ready, 1)
                    if i == 9:
                        act.wait_ge(gl_ready, layer + 1)
                        act.activation(ex[0][:, :, :], decay[:, :, :], ACT.Exp).then_inc(eg_done, 1)
                        act.activation(ex[1][:, :, :], ex[1][:, :, :], ACT.Exp).then_inc(eg_done, 1)
                    s = ORDER[i]
                    if s in (Q, V, O_G, A_G, SC):
                        dst, func, done = {
                            Q: (lambda u: qf[:, u, :], ACT.Silu, qf_ready),
                            V: (lambda u: vals[:, 2 * u:2 * u + 2, :].rearrange("p t g -> p (t g)"), ACT.Copy, v_ready),
                            O_G: (lambda u: ogate[:, 2 * u:2 * u + 2, :].rearrange("p t g -> p (t g)"), ACT.Silu, og_ready),
                            A_G: (lambda u: agate[:, u, :], ACT.Gelu_apprx_tanh, ag_ready),
                            SC: (lambda u: scv[:, u, :], ACT.Copy, sc_ready),
                        }[s]
                        for u in range(2):
                            from_ring(layer, (s, u), dst(u), func).then_inc(done, 1)
                act.wait_ge(w_used, first + N_IN)
                for r, (k, src) in enumerate(((6, scv), (0, mult))):
                    act.wait_ge(y_ready, 3 * layer + r + 1)
                    act.activation(act_hi[:, k:k + 2, :], src[:, :, :], ACT.Copy).then_inc(y_hi, 1)
                round_piece(first + N_IN + 2)
                act.wait_ge(klt_done, layer + 1)
                xflat = xs[0].rearrange("p c t -> p (c t)")
                link(act.activation(xflat[:, 0:512], ps[:, 4, :], ACT.Copy))
                act.activation(xflat[:, 512:768], ps[:, 5, 0:256], ACT.Copy).then_inc(klt_ready, 1)
                act.wait_ge(y_ready, 3 * layer + 3)
                act.activation(act_hi[:, 4:6, :], agate[:, :, :], ACT.Copy).then_inc(y_hi, 1)
                act.wait_ge(o_done, layer + 1)
                sq = ex[1].rearrange("p c t -> p (c t)")
                act.activation(sq[:, 0:512], ps[:, 7, :], ACT.Square).then_inc(osq_done, 1)
                act.activation(sq[:, 512:1024], ps[:, 4, :], ACT.Square).then_inc(osq_done, 1)
                act.wait_ge(ovar_done, layer + 1)
                act.activation(o_var, o_var, ACT.Sqrt).then_inc(osd_done, 1)
                act.wait_ge(ybt_done, layer + 1)
                for ct, bank in enumerate((4, 7)):
                    ins = act.activation(act_hi[:, 2 + ct, :], ps[:, bank, :], ACT.Copy)
                ins.then_inc(y_hi, 1)
                for j in range(1, 4 if layer == 0 else 2):
                    round_piece(first + N_IN + j + 2)

            mixers(0)
            norm(1)
            norm_evac(1)
            with act.Fori(0, DC) as c:
                def round_next(j):
                    n = DENSE0 + 3 + j
                    act.wait_ge(raw_loaded[n % 3], c * 16 + 16 * (n // 3 + 1))
                    act.wait_ge(w_used, c * 3 + (n - 2))
                    act.activation(w_his[:, n % 3, :], raw[:, n % 3, :], ACT.Copy).then_inc(w_hi_done, 1)

                round_next(-1)
                for ft in range(2):
                    if ft == 0:
                        act.wait_ge(gu_done, c * 2 + 1)
                    else:
                        act.wait_ge(w_used, c * 3 + (DENSE0 + 1))
                    act.activation(silu_d[:, ft, :], ps[:, ft, :], ACT.Silu).then_inc(s_ready, 1)

                round_next(0)
                for ft in range(2):
                    act.wait_ge(hid_ready, c * 2 + (ft + 1))
                    act.activation(hid_hi[:, ft, :], hid_d[:, ft, :], ACT.Copy).then_inc(hid_hi_sem, 1)
                round_next(1)
            mixers(1)
            norm(3)
            norm_evac(3)
            act.wait_ge(route_ready, 2)
            act.activation(rt[:, 9, 4:8], rt[:, 9, 4:8], ACT.Exp).then_inc(par_act, 1)

            slot_hi = [w_his[:, (MOE0 + j) % 3, :] for j in range(3)] + [w_hi2[:, j, :] for j in range(3)]

            def round_ahead(p, at_):
                n = MOE0 + p
                if at_ is None:
                    act.wait_ge(raw_loaded[n % 3], 16 * (n // 3 + 1))
                    act.wait_ge(w_used, MOE0)
                else:
                    act.wait_ge(raw_loaded[n % 3], at_.thirds * 16 + 16 * (n // 3 + 1))
                    act.wait_ge(w_used, at_.pieces + (n - 5))
                act.activation(slot_hi[p % 6], raw[:, n % 3, :], ACT.Copy).then_inc(w_hi_done, 1)

            def silu_block(b, at_, v, early=False):
                if early:
                    act.wait_ge(g_done, v + 1)
                else:
                    act.wait_ge(w_used, at_.pieces + (MOE0 + 3))
                act.activation(silu_e[:, b, :], ps[:, 2 * b, :], ACT.Silu).then_inc(se_ready[b], 1)

            def fold_block(at_):
                for kind in range(2):
                    act.wait_ge(w_used, at_.pieces + (MOE0 + 3 + kind))
                    act.activation(fold[0:NARROW, kind, :], ps[NARROW:P, 2 + kind, :], ACT.Copy) \
                        .then_inc(half_copied, 1)

            def silu_folded(w):
                act.wait_ge(gate_folded, w + 1)
                act.activation(silu_e[0:NARROW, 1, :], fold[0:NARROW, 0, :], ACT.Silu).then_inc(se_ready[1], 1)

            def turned(b, count):
                act.wait_ge(t_done[b], count + 1)
                act.activation(ht[:, b, :, 0, :], ps[:, 4, :].rearrange("p (f t) -> p f t", t=P), ACT.Copy) \
                    .then_inc(ht_hi_done[b], 1)

            def turned_rows(b, n):
                act.wait_ge(xt_tr, n * 2 + (b + 1))
                act.activation(xt[:, b, :, 0, :],
                               ps[:, 2 * b:2 * b + 2, :].rearrange("p a (k t) -> p (a k) t", t=P), ACT.Copy) \
                    .then_inc(xt_hi_done, 1)

            act.wait_ge(items_ready, 1)
            for i in range(2):
                act.wait_ge(hn_stored[i], 32)
            for p in range(AHEAD):
                round_ahead(p, None)
            for b in range(2):
                turned_rows(b, 0)
            n_items = act.value_load(items[0:1, 32:33], min_val=1, max_val=MAX_ITEMS)
            pairs = act.alloc_register("act_pairs")
            act.reg_mov(pairs, 0)

            narrows = act.alloc_register("act_narrows")
            act.reg_mov(narrows, 0)

            def count(register):
                return act.snap(register, min_val=0, max_val=EC * MAX_ITEMS)

            with act.Fori(0, n_items) as n:
                start_ = At(n * IP, n * (IP // 3))
                for p in range(2):
                    round_ahead(p + AHEAD, start_)
                two = act.value_load(items[0:1, bass.ds(n + 16, 1)], min_val=0, max_val=1)
                end_ = At(n * IP + 6 * (EC - 1), n * (IP // 3) + 2 * (EC - 1))
                q_end = n * EC + (EC - 1)
                narrow = act.value_load(items[0:1, bass.ds(n + 48, 1)], min_val=0, max_val=1)

                def item_two(narrow):
                    with act.Fori(0, EC - 1) as c:
                        q, v = n * EC + c, count(pairs)
                        at_ = At(n * IP + c * 6, n * (IP // 3) + c * 2)
                        silu_block(0, at_, v, early=True)
                        round_ahead(2 + AHEAD, at_)
                        if narrow:
                            w = count(narrows)
                            fold_block(at_)
                            round_ahead(3 + AHEAD, at_)
                            silu_folded(w)
                            act.reg_add(narrows, narrows, 1)
                        else:
                            round_ahead(3 + AHEAD, at_)
                            silu_block(1, at_, v)
                        if narrow:
                            turned(0, q)
                            round_ahead(4 + AHEAD, at_)
                            turned(1, v)
                            round_ahead(5 + AHEAD, at_)
                        else:
                            round_ahead(4 + AHEAD, at_)
                            round_ahead(5 + AHEAD, at_)
                            turned(0, q)
                            turned(1, v)
                        round_ahead(6 + AHEAD, at_)
                        round_ahead(7 + AHEAD, at_)
                        act.reg_add(pairs, pairs, 1)
                    v = count(pairs)
                    silu_block(0, end_, v, early=True)
                    round_ahead(2 + AHEAD, end_)
                    if narrow:
                        w = count(narrows)
                        fold_block(end_)
                        turned(0, q_end)
                        silu_folded(w)
                        act.reg_add(narrows, narrows, 1)
                    else:
                        silu_block(1, end_, v)
                        turned(0, q_end)
                    round_ahead(3 + AHEAD, end_)
                    turned(1, v)
                    for b in range(2):
                        turned_rows(b, n + 1)
                    round_ahead(4 + AHEAD, end_)
                    round_ahead(5 + AHEAD, end_)
                    act.reg_add(pairs, pairs, 1)

                with act.If(two > 0):
                    with act.If(narrow > 0):
                        item_two(True)
                    with act.Else():
                        item_two(False)
                with act.Else():
                    with act.Fori(0, EC - 1) as c:
                        q = n * EC + c
                        at_ = At(n * IP + c * 6, n * (IP // 3) + c * 2)
                        silu_block(0, at_, None)
                        round_ahead(2 + AHEAD, at_)
                        round_ahead(3 + AHEAD, at_)
                        turned(0, q)
                        for p in range(4, 8):
                            round_ahead(p + AHEAD, at_)
                    silu_block(0, end_, None)
                    round_ahead(2 + AHEAD, end_)
                    turned(0, q_end)
                    round_ahead(3 + AHEAD, end_)
                    for b in range(2):
                        turned_rows(b, n + 1)
                    round_ahead(4 + AHEAD, end_)
                    round_ahead(5 + AHEAD, end_)
            norm(4)

        @block.vector
        def _(dve):
            chain = [0]

            def link(ins):
                chain[0] += 1
                ins.then_inc(dve_chain, 1)
                dve.wait_ge(dve_chain, chain[0])

            def rest_piece(n):
                dve.wait_ge(w_hi_done, n + 1)
                dve.tensor_tensor(w_los[:, n % 3, :], raw[:, n % 3, :], f32(w_his[:, n % 3, :]), ALU.subtract) \
                    .then_inc(w_lo_done, 1)

            def norm_tile(m, i):
                dve.wait_ge(ssq_done, 4 * m + i + 1)
                dve.tensor_scalar(var[:, i:i + 1], ssq[:, i:i + 1], 1.0 / D, EPS, ALU.mult, ALU.add) \
                    .then_inc(var_done, 1)
                dve.wait_ge(sd_done, 4 * m + i + 1)
                link(dve.reciprocal(rstd[:, i:i + 1], var[:, i:i + 1]))
                if i == 0:
                    if m < 4:
                        dve.wait_ge(grow_loaded, 16 * (m + 1))
                    else:
                        dve.wait_ge(gain_loaded, 16)
                if m < 4:
                    if i >= 2 and m < 3:
                        dve.wait_ge(tr_done, 4 * m + i - 1)
                    dve.scalar_tensor_tensor(rows_of(m, i), h[:, i, :], rstd[:, i:i + 1], grow,
                                             ALU.mult, ALU.mult).then_inc(rows_done, 1)
                else:
                    if i >= 2:
                        dve.wait_ge(out_stored[i % 2], 16)
                    dve.scalar_tensor_tensor(yacc[:, i % 2, :], h[:, i, :], rstd[:, i:i + 1], growf[:, :],
                                             ALU.mult, ALU.mult).then_inc(out_rows, 1)

            def norm(m):
                for i in range(NT):
                    norm_tile(m, i)

            def norm_evac(m):
                for k in range(KT):
                    dve.wait_ge(in_hi, m * KT + k + 1)
                    dve.tensor_tensor(act_lo[:, k, :], ps[:, k, :], f32(act_hi[:, k, :]), ALU.subtract) \
                        .then_inc(in_lo, 1)

            def ring_ps(layer, key):
                output_done(dve, layer, key)
                return ps[:, bank_of(key), :]

            def coefficients(layer):
                dve.wait_ge(par_loaded, 16 * (layer + 1))
                lam = par[:, COLS["lam"]:COLS["lam"] + 2]
                lb0 = par[:, COLS["hlb"]:COLS["hlb"] + 2]
                lb1 = par[:, COLS["hlb"] + 2:COLS["hlb"] + 4]
                link(dve.tensor_scalar(tmp[:, 6:8], lam, -1.0, None, ALU.mult))
                link(dve.tensor_tensor(tmp[:, 8:10], lb0, lb1, ALU.max))
                link(dve.tensor_tensor(tmp[:, 10:12], lam, tmp[:, 6:8], ALU.min))
                link(dve.tensor_copy(tmp[:, 0:2], tmp[:, 10:12]))
                link(dve.tensor_tensor(tmp[:, 2:4], lb0, tmp[:, 8:10], ALU.subtract))
                dve.tensor_tensor(tmp[:, 4:6], lb1, tmp[:, 8:10], ALU.subtract).then_inc(par_dve, 1)
                dve.wait_ge(par_act, layer + 1)
                y, z, z2, acc = tmp[:, 0:2], tmp[:, 8:10], tmp[:, 10:12], tmp[:, 12:14]
                link(dve.tensor_scalar(z, y, 2.0, None, ALU.add))
                link(dve.reciprocal(z2, z))
                link(dve.tensor_tensor(z, y, z2, ALU.mult))
                link(dve.tensor_tensor(z2, z, z, ALU.mult))
                link(dve.tensor_scalar(acc, z2, 1.0 / 17, 1.0 / 15, ALU.mult, ALU.add))
                for d in (13, 11, 9, 7, 5, 3, 1):
                    link(dve.tensor_tensor(acc, acc, z2, ALU.mult))
                    link(dve.tensor_scalar(acc, acc, 1.0 / d, None, ALU.add))
                link(dve.tensor_tensor(acc, acc, z, ALU.mult))
                link(dve.tensor_scalar(tmp[:, 14:16], tmp[:, 6:8], 0.0, -8.0, ALU.max, ALU.mult))
                link(dve.scalar_tensor_tensor(coef, acc, -16.0, tmp[:, 14:16], ALU.mult, ALU.add))
                e0, e1 = tmp[:, 2:4], tmp[:, 4:6]
                link(dve.tensor_tensor(tmp[:, 16:18], e0, e1, ALU.add))
                link(dve.reciprocal(tmp[:, 18:20], tmp[:, 16:18]))
                link(dve.tensor_tensor(e0, e0, tmp[:, 18:20], ALU.mult))
                link(dve.tensor_tensor(e1, e1, tmp[:, 18:20], ALU.mult))
                cum = e0
                if layer:
                    link(dve.tensor_tensor(tmp[:, 16:18], e0, e1, ALU.add))
                    cum = tmp[:, 16:18]
                link(dve.tensor_tensor(lbs, cum, e0, ALU.subtract))
                dve.tensor_scalar(omlb, lbs, -1.0, 1.0, ALU.mult, ALU.add).then_inc(par_dve, 1)
                dve.wait_ge(par_dve, 2 * layer + 2)

            def views(t, half):
                v = t.rearrange("p c t -> p (c t)").rearrange("p (n x h) -> p n x h", x=2, h=half)
                return v[:, :, 0, :], v[:, :, 1, :]

            def level_exponents(layer, lv):
                half = 1 << (lv - 1)
                left, right = views(decay, half)
                e_left, e_right = views(ex[lv % 2], half)
                mid = left[:, :, half - 1:half].broadcast_to([P, CT * T // (2 * half), half])
                dve.tensor_tensor(e_left, mid, left, ALU.subtract)
                dve.tensor_tensor(e_right, right, mid, ALU.subtract).then_inc(ex_ready, 1)

            def level_operand(layer, lv):
                half = 1 << (lv - 1)
                if lv >= 3:
                    dve.wait_ge(level_done, 4 * (layer * LEVELS + lv - 1))
                dve.wait_ge(exp_done, 7 * layer + lv)
                e_left, e_right = views(ex[lv % 2], half)
                x_left, x_right = views(xs[lv % 2], half)
                k_left, _ = views(keys, half)
                _, q_right = views(qf, half)
                dve.tensor_tensor(x_left, k_left, e_left, ALU.mult)
                dve.tensor_tensor(x_right, q_right, e_right, ALU.mult).then_inc(xs_ready, 1)

            def level_keep(layer, lv):
                if layer == 0 and lv == 0:
                    dve.wait_ge(mask_ready, 1)
                m = mask[:, lv, :].unsqueeze(1).broadcast_to([P, NT, P])
                for hd in range(NH):
                    dve.wait_ge(level_done, 4 * (layer * LEVELS + lv) + hd + 1)
                    dve.copy_predicated(scores[:, hd, :, :], m, ps[:, 4 + hd, :].rearrange("p (c t) -> p c t", c=NT)) \
                        .then_inc(level_read, 1)

            def lo_of(layer, k, src):
                dve.tensor_tensor(act_lo[:, k:k + 2, :], src, f32(act_hi[:, k:k + 2, :]), ALU.subtract) \
                    .then_inc(y_lo, 1)

            def mixers(layer):
                first = layer * LAYER1
                norm(2 * layer)
                if layer == 0:
                    rest_piece(0)
                norm_evac(2 * layer)
                for n in (first + 2,) if layer else (1, 2):
                    rest_piece(n)
                coefficients(layer)
                for u in range(2):
                    src = ring_ps(layer, (FG, u))
                    ins = dve.tensor_scalar(xs[1][:, u, :], src, -1.0, 80.0, ALU.mult, ALU.min)
                    ins.then_inc(e_ready, 1)
                dve.memset(scores[:, :, :, :], 0.0).then_inc(dve_chain, 1)
                dve.memset(lru_in[:, :, 0:3], 0.0).then_inc(dve_chain, 1)
                dve.memset(sxv[:, :, 0:2], 0.0).then_inc(dve_chain, 1)
                chain[0] += 3
                dve.wait_ge(ln_ready, 2 * layer + 1)
                for ct in range(CT):
                    ins = dve.tensor_scalar(keys[:, ct, :], keys[:, ct, :], omlb[:, ct:ct + 1], None, ALU.mult)
                ins.then_inc(xs_ready, 1)
                dve.wait_ge(ln_ready, 2 * layer + 2)
                link(dve.tensor_tensor(xs[0][:, :, :], ex[0][:, :, :], ex[1][:, :, :], ALU.subtract))
                for ct in range(CT):
                    for c in range(NT):
                        lf = xs[0][:, ct, c * P:(c + 1) * P]
                        ins = dve.tensor_tensor_scan(decay[:, ct, c * P:(c + 1) * P], lf, lf, 0.0, ALU.add, ALU.min)
                link(ins)
                for i in range(1, N_IN):
                    rest_piece(first + i + 2)
                    if i < LEVELS:
                        if i >= 3:
                            dve.wait_ge(xs_ready, layer * LEVELS + i - 1)
                        level_exponents(layer, i)
                    if i == 2:
                        dve.wait_ge(qf_ready, 2 * layer + 2)
                    if 1 <= i - 1 < LEVELS:
                        level_operand(layer, i - 1)
                    if i >= 3:
                        level_keep(layer, i - 3)
                    if i == 4:
                        dve.wait_ge(dve_chain, chain[0])
                        for ct in range(CT):
                            link(dve.tensor_scalar(x_in[:, ct, :], lru_in[:, ct, 3:3 + T], pcol("conv_w", 6 + ct),
                                                   pcol("conv_b", ct), ALU.mult, ALU.add))
                            for j in (2, 1, 0):
                                ins = dve.scalar_tensor_tensor(
                                    x_in[:, ct, :], lru_in[:, ct, j:j + T], pcol("conv_w", 2 * j + ct),
                                    x_in[:, ct, :], ALU.mult, ALU.add)
                                if j or ct == 0:
                                    link(ins)
                        ins.then_inc(xin_ready, 1)
                    if i == 6:
                        dve.wait_ge(og_ready, 2 * layer + 2)
                        g = par[:, COLS["norm_g"]:COLS["norm_g"] + GW].unsqueeze(1).broadcast_to([P, NT, GW])
                        link(dve.tensor_tensor(ogate[:, :, :], ogate[:, :, :], g, ALU.mult))
                    if i == 8:
                        if layer:
                            dve.wait_ge(y_zeroed, 16)
                        dve.wait_ge(ta_ready, 4 * (layer + 1))
                        link(dve.tensor_tensor(mult[:, :, :], r_gate, r_gate, ALU.mult))
                        dve.scalar_tensor_tensor(mult[:, :, :], mult[:, :, :], 1.0, tanh_l, ALU.add, ALU.mult) \
                            .then_inc(m2_ready, 1)
                        link(dve.tensor_tensor(igate[:, :, :], igate[:, :, :], x_in, ALU.mult))
                        for ct in range(CT):
                            link(dve.tensor_scalar(scv[:, ct, :], sxv[:, ct, 2:2 + T], pcol("sconv_w", 4 + ct),
                                                   None, ALU.mult))
                            for j in (1, 0):
                                link(dve.scalar_tensor_tensor(
                                    scv[:, ct, :], sxv[:, ct, j:j + T], pcol("sconv_w", 2 * j + ct),
                                    scv[:, ct, :], ALU.mult, ALU.add))
                        dve.wait_ge(mult_ready, layer + 1)
                        link(dve.tensor_tensor(igate[:, :, :], igate[:, :, :], mult[:, :, :], ALU.mult))
                        for ct in range(CT):
                            ins = dve.tensor_tensor_scan(mult[:, ct, :], r_gate[:, ct, :], igate[:, ct, :], 0.0,
                                                         ALU.mult, ALU.add)
                            link(ins)
                        dve.wait_ge(ag_ready, 2 * layer + 2)
                        link(dve.tensor_tensor(mult[:, :, :], mult[:, :, :], agate[:, :, :], ALU.mult))
                        link(dve.memset(lru_in[:, :, 0:16], 0.0))
                    if i == 9:
                        last = decay[:, :, :].rearrange("p c (n t) -> p (c n) t", t=P)
                        dve.tensor_tensor(ex[1].rearrange("p c (n t) -> p (c n) t", t=P),
                                          last[:, :, P - 1:P].broadcast_to([P, CT * NT, P]), last,
                                          ALU.subtract).then_inc(gl_ready, 1)
                    s = ORDER[i]
                    if s == A_X:
                        for u in range(2):
                            ins = dve.tensor_copy(lru_in[:, u, 3:3 + T], ring_ps(layer, (s, u)))
                            ins.then_inc(ax_read, 1)
                        dve.wait_ge(ax_read, 2 * (layer + 1))
                    elif s == SX:
                        dve.wait_ge(sc_ready, 2 * layer + 2)
                        for u in range(2):
                            ins = dve.tensor_tensor(sxv[:, u, 2:2 + T], ring_ps(layer, (s, u)), scv[:, u, :], ALU.mult)
                            ins.then_inc(sx_read, 1)
                        dve.wait_ge(sx_read, 2 * (layer + 1))
                    elif s == SB:
                        for u in range(2):
                            ins = dve.tensor_tensor(scv[:, u, :], ring_ps(layer, (s, u)), scv[:, u, :], ALU.mult)
                            ins.then_inc(sb_read, 1)
                        dve.wait_ge(sb_read, 2 * (layer + 1))
                        dve.sem_inc(y_ready, 1)
                        dve.sem_inc(y_ready, 1)
                    elif s == PL:
                        for u in range(2):
                            ins = dve.tensor_copy(lru_in[:, u, 16:16 + T], ring_ps(layer, (s, u)))
                            ins.then_inc(pl_read, 1)
                        dve.wait_ge(pl_read, 2 * (layer + 1))
                dve.wait_ge(eg_done, 2 * (layer + 1))
                link(dve.tensor_copy(eg_last, ex[0].rearrange("p c (n t) -> p c n t", t=P)[:, :, :, P - 1]))
                dve.tensor_tensor(ex[1][:, :, :], keys[:, :, :], ex[1][:, :, :], ALU.mult).then_inc(kl_ready, 1)
                link(dve.tensor_tensor(ex[0][:, :, :], qf[:, :, :], ex[0][:, :, :], ALU.mult))
                for r, (k, src) in enumerate(((6, scv), (0, mult))):
                    dve.wait_ge(y_hi, 4 * layer + r + 1)
                    lo_of(layer, k, src[:, :, :])
                level_keep(layer, 7)
                N = T + 16
                link(dve.tensor_tensor(w1b[:, :, 1:N], lru_in[:, :, 1:N], lru_in[:, :, 0:N - 1], ALU.add))
                link(dve.tensor_tensor(w2b[:, :, 3:N], w1b[:, :, 3:N], w1b[:, :, 1:N - 2], ALU.add))
                link(dve.tensor_tensor(w1b[:, 1, 7:N], w2b[:, 1, 7:N], w2b[:, 1, 3:N - 4], ALU.add))
                link(dve.tensor_tensor(w2b[:, 1, 15:N], w1b[:, 1, 15:N], w1b[:, 1, 7:N - 8], ALU.add))
                ramp = par[:, COLS["ramp"]:COLS["ramp"] + 32].rearrange("p (c t) -> p c t", c=2)
                for lo, w in ((0, w1b), (HD, w2b)):
                    link(dve.tensor_tensor(w[lo:lo + HD, :, 16:32], w[lo:lo + HD, :, 16:32], ramp[lo:lo + HD], ALU.mult))
                for ct in range(CT):
                    for lo, w in ((0, w1b), (HD, w2b)):
                        win = 2 << (2 * ct + lo // HD)
                        ins = dve.scalar_tensor_tensor(
                            igate[lo:lo + HD, ct, :], w[lo:lo + HD, ct, 16:N], 1.0 / win,
                            lru_in[lo:lo + HD, ct, 16:N], ALU.mult, ALU.subtract)
                        if (ct, lo) != (1, HD):
                            link(ins)
                ins.then_inc(pd_ready, 1)
                rest_piece(first + N_IN + 2)
                dve.wait_ge(ds_done, layer + 1)
                for c in range(NT - 1):
                    for ct in range(CT):
                        d_s = ps[:, 6, c * P + ct * HD:c * P + (ct + 1) * HD]
                        if c == 0:
                            ins = dve.tensor_copy(state[:, 1, ct, :], d_s)
                        else:
                            ins = dve.scalar_tensor_tensor(state[:, c + 1, ct, :], state[:, c, ct, :],
                                                           eg_last[:, ct, c:c + 1], d_s, ALU.mult, ALU.add)
                    ins.then_inc(st_ready, 1)
                    dve.wait_ge(st_ready, (NT - 1) * layer + c + 1)
                for u in range(2):
                    dve.wait_ge(pool_done, 2 * layer + u + 1)
                    ins = dve.tensor_scalar(agate[:, u, :], ps[:, 5 + u, :], pcol("pool_scale", u),
                                            None, ALU.mult)
                    if u == 0:
                        link(ins)
                ins.then_inc(y_ready, 1)
                dve.wait_ge(y_hi, 4 * layer + 3)
                lo_of(layer, 4, agate[:, :, :])
                dve.wait_ge(osq_done, 2 * (layer + 1))
                link(dve.tensor_reduce(o_ssq, ex[1].rearrange("p c t -> p (c t)").rearrange("p (n v) -> p n v", v=HD),
                                       AX.X, ALU.add))
                dve.tensor_scalar(o_var, o_ssq, 1.0 / HD, HEAD_EPS, ALU.mult, ALU.add).then_inc(ovar_done, 1)
                dve.wait_ge(osd_done, layer + 1)
                link(dve.reciprocal(o_rstd, o_var))
                on = xs[1].rearrange("p c t -> p (c t)")
                by_parity = on.rearrange("p (n b v) -> p n b v", b=2, v=HD)
                for half, bank in ((0, 7), (1, 4)):
                    link(dve.tensor_tensor(
                        by_parity[:, :, half, :],
                        ps[:, bank, :].rearrange("p (n v) -> p n v", v=HD),
                        o_rstd[:, half * 8:(half + 1) * 8].unsqueeze(2).broadcast_to([P, 8, HD]), ALU.mult))
                dve.tensor_tensor(on, on, ogate.rearrange("p n g -> p (n g)"), ALU.mult).then_inc(on_ready, 1)
                dve.wait_ge(y_hi, 4 * layer + 4)
                for ct, bank in enumerate((4, 7)):
                    ins = dve.tensor_tensor(act_lo[:, 2 + ct, :], ps[:, bank, :], f32(act_hi[:, 2 + ct, :]),
                                            ALU.subtract)
                ins.then_inc(y_lo, 1)
                for j in range(1, 4 if layer == 0 else 2):
                    rest_piece(first + N_IN + j + 2)
                for half in range(2):
                    s_ = slice(half * 512, (half + 1) * 512)
                    for tt in range(NT):
                        if tt < NT - 1:
                            dve.wait_ge(out_done, 3 * (4 * layer + 2 * half + 1) + tt + 1)
                        else:
                            dve.wait_ge(w_used, first + N_IN + 2 * half + 2)
                        ins = dve.tensor_tensor(h[:, tt, s_], h[:, tt, s_], ps[:, tt + 4 * half, :], ALU.add)
                        if half:
                            ins.then_inc(h_ready, 1)
                            for i in ((0,), (1,), (), (2, 3))[tt]:
                                norm_tile(2 * layer + 1, i)
                        else:
                            link(ins)

            mixers(0)
            norm_evac(1)
            dve.sem_inc(down_added, 4)
            with dve.Fori(0, DC) as c:
                def rest_next(j):
                    n = DENSE0 + 3 + j
                    dve.wait_ge(w_hi_done, c * 3 + (n + 1))
                    dve.tensor_tensor(w_los[:, n % 3, :], raw[:, n % 3, :], f32(w_his[:, n % 3, :]), ALU.subtract) \
                        .then_inc(w_lo_done, 1)

                rest_next(-1)
                for ft in range(2):
                    dve.wait_ge(s_ready, c * 2 + (ft + 1))
                    if ft == 0:
                        dve.wait_ge(gu_done, c * 2 + 2)
                    else:
                        dve.wait_ge(w_used, c * 3 + (DENSE0 + 2))
                    dve.tensor_tensor(hid_d[:, ft, :], silu_d[:, ft, :], ps[:, 2 + ft, :], ALU.mult) \
                        .then_inc(hid_ready, 1)
                    dve.wait_ge(hid_hi_sem, c * 2 + (ft + 1))
                    dve.tensor_tensor(hid_lo[:, ft, :], hid_d[:, ft, :], f32(hid_hi[:, ft, :]), ALU.subtract) \
                        .then_inc(hid_lo_ready, 1)
                rest_next(0)
                for tt in range(NT):
                    if tt == 2:
                        rest_next(1)
                    if tt < NT - 1:
                        dve.wait_ge(down_done, c * 3 + (tt + 1))
                    else:
                        dve.wait_ge(w_used, c * 3 + (DENSE0 + 3))
                    b = 4 + 2 * (tt % 2)
                    dve.tensor_tensor(h[:, tt, :], h[:, tt, :], ps[:, b:b + 2, :].rearrange("p a d -> p (a d)"),
                                      ALU.add).then_inc(down_added, 1)
            mixers(1)
            dve.wait_ge(moe_const_loaded, 32)
            dve.tensor_copy(wr_hi[:, :, :], wr[:, :, :]).then_inc(wr_split, 1)
            dve.wait_ge(wr_split, 1)
            dve.tensor_tensor(wr_lo[:, :, :], wr[:, :, :], f32(wr_hi[:, :, :]), ALU.subtract).then_inc(wr_split, 1)
            norm_evac(3)

            dve.wait_ge(logits_turned, 1)
            dve.tensor_copy(fold[0:NE, 0, :], ps[0:NE, 0, :]).then_inc(logits_copied, 1)
            dve.wait_ge(logits_done, 1)

            def r3(i):
                return rt[:, i, :].rearrange("p (t e) -> p t e", e=NE)

            def wide(ap):
                return ap.unsqueeze(2).broadcast_to([P, NT, NE])

            def per_e(ap):
                return ap.unsqueeze(1).broadcast_to([P, NT, NE])

            LG, EQ, CAND, OH1, OH2, LG2, SLOT, PROD, CH, SM, RK, ST = range(12)
            iota8 = mcon[:, MC_IOTA:MC_IOTA + NE]
            m1, m2, first_e = rt[:, SM, 0:4], rt[:, SM, 4:8], rt[:, SM, 8:12]
            link(dve.tensor_copy(rt[:, LG, :], ps[:, 1, 0:NT * NE]))

            def choose(lg, best, oh):
                link(dve.tensor_reduce(best, r3(lg), AX.X, ALU.max))
                link(dve.tensor_tensor(r3(EQ), r3(lg), wide(best), ALU.is_equal))
                link(dve.tensor_tensor(r3(CAND), r3(EQ), per_e(iota8), ALU.mult))
                link(dve.tensor_reduce(first_e, r3(CAND), AX.X, ALU.min))
                link(dve.tensor_tensor(r3(oh), per_e(iota8), wide(first_e), ALU.is_equal))

            choose(LG, m1, OH1)
            link(dve.scalar_tensor_tensor(rt[:, LG2, :], rt[:, OH1, :], -1e30, rt[:, LG, :], ALU.mult, ALU.add))
            choose(LG2, m2, OH2)
            dve.tensor_tensor(rt[:, CH, :], rt[:, OH1, :], rt[:, OH2, :], ALU.add).then_inc(route_ready, 1)
            dve.tensor_tensor(rt[:, 9, 4:8], m2, m1, ALU.subtract).then_inc(route_ready, 1)
            dve.wait_ge(par_act, DEPTH + 1)
            g1, g2 = rt[:, 12, 0:4], rt[:, 12, 4:8]
            link(dve.tensor_scalar(rt[:, 12, 8:12], rt[:, 9, 4:8], 1.0, None, ALU.add))
            link(dve.reciprocal(g1, rt[:, 12, 8:12]))
            link(dve.tensor_tensor(g2, rt[:, 9, 4:8], g1, ALU.mult))
            dve.wait_ge(rank_done, 1)
            cnt, n_of, incl, start = (rt[:, 13, 8 * i:8 * i + 8] for i in range(4))
            has2 = rt[:, 14, 0:8]
            has1 = rt[:, 14, 8:16]
            link(dve.tensor_copy(rt[:, RK, :], ps[:, 3, 0:NT * NE]))
            link(dve.tensor_copy(cnt, ps[:, 2, 0:NE]))
            link(dve.tensor_scalar(has1, cnt, 0.0, None, ALU.is_gt))
            link(dve.tensor_scalar(has2, cnt, float(ROWS), None, ALU.is_gt))
            link(dve.tensor_tensor(n_of, has1, has2, ALU.add))
            link(dve.tensor_tensor_scan(incl, n_of, mcon[:, MC_ZERO:MC_ZERO + NE], 0.0, ALU.add, ALU.add))
            link(dve.tensor_tensor(start, incl, n_of, ALU.subtract))
            link(dve.tensor_scalar(rt[:, 15, 0:8], start, float(ROWS), None, ALU.mult))
            link(dve.tensor_tensor(r3(SLOT), r3(RK), per_e(rt[:, 15, 0:8]), ALU.add))
            for j, oh in enumerate((OH1, OH2)):
                link(dve.tensor_tensor(r3(PROD), r3(SLOT), r3(oh), ALU.mult))
                link(dve.tensor_reduce(rt[:, 16, 4 * j:4 * j + 4], r3(PROD), AX.X, ALU.add))
                link(dve.tensor_copy(slots[:, :, j], rt[:, 16, 4 * j:4 * j + 4]))
            dve.tensor_copy(tokens[:, :], mcon[:, MC_TOK:MC_TOK + NT]).then_inc(slots_ready, 1)
            w3v = [rtw[0:1, i, :].rearrange("p (n e) -> p n e", e=NE) for i in range(5)]

            def over_n(ap):
                return ap.unsqueeze(1).broadcast_to([1, 16, NE])

            n_row = mcon[0:1, MC_N:MC_N + 128].rearrange("p (n e) -> p n e", e=NE)
            e_row = mcon[0:1, MC_E:MC_E + NE]
            s1 = rt[0:1, 17, 0:8]
            over1, over2 = rt[0:1, 17, 8:16], rt[0:1, 17, 16:24]
            fits1, fits2 = rt[0:1, 17, 24:32], rt[0:1, 14, 16:24]
            link(dve.tensor_scalar(s1, start[0:1], 1.0, None, ALU.add))
            link(dve.tensor_scalar(over1, cnt[0:1], float(P), None, ALU.is_gt))
            link(dve.tensor_scalar(over2, cnt[0:1], float(ROWS + P), None, ALU.is_gt))
            link(dve.tensor_tensor(w3v[0], n_row, over_n(start[0:1]), ALU.is_equal))
            link(dve.tensor_tensor(w3v[0], w3v[0], over_n(has1[0:1]), ALU.mult))
            link(dve.tensor_tensor(w3v[1], n_row, over_n(s1), ALU.is_equal))
            link(dve.tensor_tensor(w3v[1], w3v[1], over_n(has2[0:1]), ALU.mult))
            link(dve.tensor_tensor(w3v[2], w3v[0], w3v[1], ALU.add))
            link(dve.tensor_tensor(w3v[2], w3v[2], over_n(e_row), ALU.mult))
            link(dve.tensor_reduce(rt[0:1, 18, 0:16], w3v[2], AX.X, ALU.add))
            link(dve.tensor_scalar(fits1, cnt[0:1], float(P + NARROW), None, ALU.is_le))
            link(dve.tensor_scalar(fits2, cnt[0:1], float(ROWS + P + NARROW), None, ALU.is_le))
            link(dve.tensor_tensor(w3v[0], w3v[0], over_n(over1), ALU.mult))
            link(dve.tensor_tensor(w3v[1], w3v[1], over_n(over2), ALU.mult))
            link(dve.tensor_tensor(w3v[3], w3v[0], over_n(fits1), ALU.mult))
            link(dve.tensor_tensor(w3v[4], w3v[1], over_n(fits2), ALU.mult))
            link(dve.tensor_tensor(w3v[3], w3v[3], w3v[4], ALU.add))
            link(dve.tensor_reduce(rt[0:1, 16, 8:24], w3v[3], AX.X, ALU.add))
            link(dve.tensor_copy(items[0:1, 48:64], rt[0:1, 16, 8:24]))
            link(dve.tensor_tensor(w3v[2], w3v[0], w3v[1], ALU.add))
            link(dve.tensor_reduce(rt[0:1, 18, 16:32], w3v[2], AX.X, ALU.add))
            link(dve.tensor_scalar(rt[0:1, 19, 0:16], rt[0:1, 18, 16:32], 2.0 * EC, 2.0 * EC, ALU.mult, ALU.add))
            link(dve.tensor_scalar(rt[0:1, 19, 16:32], rt[0:1, 18, 16:32], 0.0, None, ALU.mult))
            link(dve.tensor_tensor_scan(rtw[0:1, 3, 0:16], rt[0:1, 19, 0:16], rt[0:1, 19, 16:32], 0.0,
                                        ALU.add, ALU.add))
            link(dve.tensor_copy(items[0:1, 33:48], rtw[0:1, 3, 0:15]))
            link(dve.tensor_copy(items[0:1, 32:33], incl[0:1, NE - 1:NE]))
            dve.tensor_copy(items[0:1, 0:32], rt[0:1, 18, :]).then_inc(items_ready, 1)
            dve.wait_ge(items_ready, 1)

            slot_hi = [w_his[:, (MOE0 + j) % 3, :] for j in range(3)] + [w_hi2[:, j, :] for j in range(3)]
            slot_lo = [w_los[:, (MOE0 + j) % 3, :] for j in range(3)] + [w_lo2[:, j, :] for j in range(3)]

            def rest_ahead(p, at_):
                n = MOE0 + p
                dve.wait_ge(w_hi_done, n + 1 if at_ is None else at_ + (n + 1))
                dve.tensor_tensor(slot_lo[p % 6], raw[:, n % 3, :], f32(slot_hi[p % 6]), ALU.subtract) \
                    .then_inc(w_lo_done, 1)

            def hidden(b, count, at_, v, early=False):
                dve.wait_ge(se_ready[b], count + 1)
                if early:
                    dve.wait_ge(u_done, v + 1)
                else:
                    dve.wait_ge(w_used, at_ + (MOE0 + 4))
                dve.tensor_tensor(hid_e[:, b, :], silu_e[:, b, :], ps[:, 2 * b + 1, :], ALU.mult) \
                    .then_inc(he_ready[b], 1)

            def turned(b, count):
                dve.wait_ge(ht_hi_done[b], count + 1)
                dve.tensor_tensor(ht[:, b, :, 1, :], ps[:, 4, :].rearrange("p (f t) -> p f t", t=P),
                                  f32(ht[:, b, :, 0, :]), ALU.subtract) \
                    .then_inc(ht_lo_done[b], 1)

            def turned_rows(b, n):
                dve.wait_ge(xt_hi_done, n * 2 + (b + 1))
                dve.tensor_tensor(xt[:, b, :, 1, :],
                                  ps[:, 2 * b:2 * b + 2, :].rearrange("p a (k t) -> p (a k) t", t=P),
                                  f32(xt[:, b, :, 0, :]), ALU.subtract) \
                    .then_inc(xt_lo_done, 1)

            def add(b, half, q, v, used=None):
                bank = ((5, 6), (7, 5))[b][half]
                if used is not None:
                    dve.wait_ge(w_used, used + MOE0)
                else:
                    dve.wait_ge(ye_done, v * 2 + q + (2 * b + half + 1))
                s_ = slice(half * 512, (half + 1) * 512)
                dve.tensor_tensor(yacc[:, b, s_], yacc[:, b, s_], ps[:, bank, :], ALU.add).then_inc(ye_added, 1)

            for p in range(AHEAD):
                rest_ahead(p, None)
            for b in range(2):
                turned_rows(b, 0)
            dve.sem_inc(ye_added, 1)
            n_items = dve.value_load(items[0:1, 32:33], min_val=1, max_val=MAX_ITEMS)
            pairs = dve.alloc_register("dve_pairs")
            dve.reg_mov(pairs, 0)
            narrows = dve.alloc_register("dve_narrows")
            dve.reg_mov(narrows, 0)

            def count(register):
                return dve.snap(register, min_val=0, max_val=EC * MAX_ITEMS)

            def fold_gate(w):
                dve.wait_ge(half_copied, w * 2 + 1)
                dve.tensor_tensor(fold[0:NARROW, 0, :], fold[0:NARROW, 0, :], ps[0:NARROW, 2, :], ALU.add) \
                    .then_inc(gate_folded, 1)

            def fold_up(v, w):
                dve.wait_ge(half_copied, w * 2 + 2)
                dve.tensor_tensor(fold[0:NARROW, 1, :], fold[0:NARROW, 1, :], ps[0:NARROW, 3, :], ALU.add) \
                    .then_inc(up_folded, 1)
                dve.wait_ge(up_folded, w + 1)
                dve.wait_ge(se_ready[1], v + 1)
                dve.tensor_tensor(hid_e[0:NARROW, 1, :], silu_e[0:NARROW, 1, :], fold[0:NARROW, 1, :], ALU.mult) \
                    .then_inc(he_ready[1], 1)

            with dve.Fori(0, n_items) as n:
                for p in range(2):
                    rest_ahead(p + AHEAD, n * IP)
                two = dve.value_load(items[0:1, bass.ds(n + 16, 1)], min_val=0, max_val=1)
                end_ = n * IP + 6 * (EC - 1)
                q_end = n * EC + (EC - 1)
                narrow = dve.value_load(items[0:1, bass.ds(n + 48, 1)], min_val=0, max_val=1)

                def item_two(narrow):
                    with dve.Fori(0, EC - 1) as c:
                        q, v = n * EC + c, count(pairs)
                        at_ = n * IP + c * 6
                        hidden(0, q, at_, v, early=True)
                        rest_ahead(2 + AHEAD, at_)
                        if narrow:
                            w = count(narrows)
                            fold_gate(w)
                            fold_up(v, w)
                            dve.reg_add(narrows, narrows, 1)
                            rest_ahead(3 + AHEAD, at_)
                        else:
                            rest_ahead(3 + AHEAD, at_)
                            hidden(1, v, at_, v)
                        if narrow:
                            turned(0, q)
                            rest_ahead(4 + AHEAD, at_)
                            turned(1, v)
                            rest_ahead(5 + AHEAD, at_)
                        else:
                            rest_ahead(4 + AHEAD, at_)
                            rest_ahead(5 + AHEAD, at_)
                            turned(0, q)
                            turned(1, v)
                        dve.wait_ge(yacc_free, n + 1)
                        add(0, 0, q, v)
                        rest_ahead(6 + AHEAD, at_)
                        add(0, 1, q, v)
                        add(1, 0, q, v)
                        rest_ahead(7 + AHEAD, at_)
                        add(1, 1, q, v, used=at_ + 8)
                        dve.reg_add(pairs, pairs, 1)
                    v = count(pairs)
                    hidden(0, q_end, end_, v, early=True)
                    rest_ahead(2 + AHEAD, end_)
                    if narrow:
                        w = count(narrows)
                        fold_gate(w)
                        turned(0, q_end)
                        fold_up(v, w)
                        dve.reg_add(narrows, narrows, 1)
                    else:
                        hidden(1, v, end_, v)
                        turned(0, q_end)
                    rest_ahead(3 + AHEAD, end_)
                    turned(1, v)
                    for b in range(2):
                        turned_rows(b, n + 1)
                    add(0, 0, q_end, v)
                    add(0, 1, q_end, v)
                    rest_ahead(4 + AHEAD, end_)
                    add(1, 0, q_end, v)
                    rest_ahead(5 + AHEAD, end_)
                    add(1, 1, q_end, v, used=end_ + 6)
                    dve.reg_add(pairs, pairs, 1)

                with dve.If(two > 0):
                    with dve.If(narrow > 0):
                        item_two(True)
                    with dve.Else():
                        item_two(False)
                with dve.Else():
                    v = dve.snap(pairs, min_val=0, max_val=EC * MAX_ITEMS)
                    with dve.Fori(0, EC - 1) as c:
                        q = n * EC + c
                        at_ = n * IP + c * 6
                        hidden(0, q, at_, v)
                        rest_ahead(2 + AHEAD, at_)
                        rest_ahead(3 + AHEAD, at_)
                        turned(0, q)
                        for p in range(4, 7):
                            rest_ahead(p + AHEAD, at_)
                        dve.wait_ge(yacc_free, n + 1)
                        add(0, 0, q, v)
                        rest_ahead(7 + AHEAD, at_)
                        add(0, 1, q, v, used=at_ + 8)
                    hidden(0, q_end, end_, v)
                    rest_ahead(2 + AHEAD, end_)
                    turned(0, q_end)
                    rest_ahead(3 + AHEAD, end_)
                    for b in range(2):
                        turned_rows(b, n + 1)
                    rest_ahead(4 + AHEAD, end_)
                    add(0, 0, q_end, v)
                    rest_ahead(5 + AHEAD, end_)
                    add(0, 1, q_end, v, used=end_ + 6)

            dve.wait_ge(yacc_free, n_items + 1)

            for i in range(NT):
                for j, g in enumerate((g1, g2)):
                    dve.wait_ge(comb_loaded[2 * i + j], 16)
                    ins = dve.scalar_tensor_tensor(h[:, i, :], comb[2 * i + j][:, :], g[:, i:i + 1], h[:, i, :],
                                                   ALU.mult, ALU.add)
                    if j:
                        ins.then_inc(h_ready, 1)
                    else:
                        link(ins)
                norm_tile(4, i)


_INS = ["x", "w_in", "w_out", "ffn_w_gate", "ffn_w_up", "ffn_w_down", "moe_w_router", "moe_w1",
        "moe_w3", "moe_w2", "norm_rows", "params", "ident", "masks", "moe_const", "zeros"]


def lay_out(inputs):
    a = {k: np.ascontiguousarray(v) for k, v in inputs.items()}

    def cols(v):
        return v.reshape(-1, P).T

    packed = []
    for layer in range(DEPTH):
        par = np.zeros((P, NPAR), np.float32)

        def put(name, v):
            par[:, COLS[name]:COLS[name] + v.shape[1]] = v

        put("conv_w", cols(a["lru_conv_w"][layer]))
        put("conv_b", cols(a["lru_conv_b"][layer]))
        put("b_a", cols(a["lru_b_a"][layer]))
        put("b_x", cols(a["lru_b_x"][layer]))
        put("lam", cols(a["lru_lambda"][layer]))
        put("hlb", cols(a["hgrn_lower_bounds"]))
        put("pool_scale", cols(a["pool_scale"][layer]))
        put("sconv_w", cols(a["sconv_w"][layer]))
        put("norm_g", np.broadcast_to(np.tile(a["hgrn_norm_g"][layer], NH), (P, GW)))
        for name, w in (("bd_a", a["lru_w_a"]), ("bd_x", a["lru_w_x"]), ("bd_p", a["pool_w"])):
            for hd in range(NH):
                lo, ct = HD * (hd % 2), hd // 2
                c0 = COLS[name] + ct * P + lo
                par[lo:lo + HD, c0:c0 + HD] = w[layer, hd]
        for ct in range(CT):
            for half in range(2):
                win = 2 << (2 * ct + half)
                ramp = [win / min(t + 1, win) for t in range(16)]
                par[half * HD:(half + 1) * HD, COLS["ramp"] + ct * 16:COLS["ramp"] + (ct + 1) * 16] = ramp
        packed.append(par)

    masks = np.zeros((P, LEVELS, P), np.float32)
    s, t = np.arange(P)[:, None], np.arange(P)[None, :]
    masks[:, 0] = s == t
    for lv in range(1, LEVELS):
        half = 1 << (lv - 1)
        masks[:, lv] = (s // (2 * half) == t // (2 * half)) & (s // half % 2 == 0) & (t // half % 2 == 1)

    mc = np.zeros((P, NMC), np.float32)
    mc[:, MC_ONES:MC_ONES + P] = 1
    mc[:, MC_LOWER:MC_LOWER + P] = s < t
    mc[:, MC_IOTA:MC_IOTA + NE] = np.arange(NE) - NE
    mc[:, MC_TOK:MC_TOK + NT] = s + P * np.arange(NT)
    mc[:, MC_N:MC_N + 128] = np.arange(128) // NE
    mc[:, MC_E:MC_E + NE] = np.arange(NE)
    norm_rows = np.stack([a["norm_mix_g"][0], a["norm_ffn_g"][0], a["norm_mix_g"][1], a["norm_ffn_g"][1],
                          a["final_norm_g"]])
    a.update(norm_rows=norm_rows, params=np.stack(packed), ident=np.eye(P, dtype=np.float32), masks=masks,
             moe_const=mc, zeros=np.zeros(((2 * MAX_ITEMS + 2) * P, 1), np.uint32))
    return {k: a[k] for k in _INS}


def kernel(**inputs):
    import concourse.bacc as _bacc
    from concourse.bass_utils import run_bass_kernel_spmd as _run

    nc = _bacc.Bacc("TRN2", target_bir_lowering=False, num_devices=1)
    arrays, args = {}, []
    for name, a in lay_out(inputs).items():
        a = np.ascontiguousarray(a)
        arrays[f"in_{name}_dram"] = a
        args.append(nc.dram_tensor(f"in_{name}_dram", a.shape, mybir.dt.from_np(a.dtype), kind="ExternalInput").ap())
    args.append(nc.dram_tensor("out_0_dram", (1, T, D), F32, kind="ExternalOutput").ap())
    build(nc, *args)
    r = _run(nc, [arrays], core_ids=[0])
    return r.results[0]["out_0_dram"]
```
